# Optimizing a Trainium2 kernel written in Bass

```python
import math
import jax, jax.numpy as jnp
from jax import lax
import numpy as np

D_MODEL = 2048
BATCH = 1
SEQ = 512
DEPTH = 1
DEC_BATCH = 8
DEC_SEQ = 1
PAST_LEN = 256
PAGE_SIZE = 128

HEAD_DIM = 64
N_HEADS = 16
D_ATTN = N_HEADS * HEAD_DIM
D_CONV = D_MODEL - D_ATTN
CONV_W = 3
DIL_STEPS = 128
DILATIONS = (1, 4, 16)
WINDOWS = tuple(DIL_STEPS * d for d in DILATIONS)
W_MAX = max(WINDOWS)
N_BUCKETS = 32
MAX_EXACT = N_BUCKETS // 2
MAX_DIST = W_MAX
D_FF = ((8 * D_MODEL + 2) // 3 + 255) // 256 * 256
D_PLE = 256
EPS = 1e-6
SPLITS = [D_ATTN, 2 * D_ATTN, 3 * D_ATTN, 3 * D_ATTN + D_CONV, 3 * D_ATTN + 2 * D_CONV]
D_IN = 3 * D_ATTN + 3 * D_CONV

kernel_name = "hymba_dilated_swa_shortconv_step"

def rms_norm(x, g):
    xf = x.astype(jnp.float32)
    y = xf * lax.rsqrt(jnp.mean(xf * xf, axis=-1, keepdims=True) + EPS)
    return (y * g.astype(jnp.float32)).astype(x.dtype)

def t5_bucket(dist):
    n = np.asarray(dist, np.int32)
    nf = np.maximum(n, 1).astype(np.float32)
    large = MAX_EXACT + (np.log(nf / MAX_EXACT) / np.float32(math.log(MAX_DIST / MAX_EXACT))
                         * (N_BUCKETS - MAX_EXACT)).astype(np.int32)
    large = np.minimum(large, N_BUCKETS - 1)
    return np.where(n < MAX_EXACT, n, large).astype(np.int32)

def merge_dilations(outs, maxes, dens):
    m_all = functools_max(maxes)
    ws = [den * jnp.exp(m - m_all) for m, den in zip(maxes, dens)]
    total = sum(ws)
    return sum(w[..., None] * o for w, o in zip(ws, outs)) / total[..., None]

def functools_max(arrs):
    out = arrs[0]
    for a in arrs[1:]:
        out = jnp.maximum(out, a)
    return out

def dilated_attention_prompt(q, k, v, rel_bias):
    B, S = q.shape[:2]
    span = max(DILATIONS) * DIL_STEPS
    Tp = -(-S // span) * span
    pad = ((0, 0), (0, Tp - S), (0, 0), (0, 0))
    qp, kp, vp = jnp.pad(q, pad), jnp.pad(k, pad), jnp.pad(v, pad)
    scale = HEAD_DIM ** -0.5
    qi = np.arange(DIL_STEPS)[:, None]
    kj = np.arange(2 * DIL_STEPS)[None, :]
    steps = DIL_STEPS + qi - kj
    band = (steps >= 0) & (steps <= DIL_STEPS)
    outs, maxes, dens = [], [], []
    for d in DILATIONS:
        L = Tp // d
        nb = L // DIL_STEPS

        def to_blocks(a):
            return a.reshape(B, L, d, N_HEADS, HEAD_DIM).transpose(0, 2, 1, 3, 4).reshape(
                B, d, nb, DIL_STEPS, N_HEADS, HEAD_DIM)

        def with_prev(a):
            prev = jnp.pad(a[:, :, :-1], ((0, 0), (0, 0), (1, 0), (0, 0), (0, 0), (0, 0)))
            return jnp.concatenate([prev, a], axis=3)

        def from_blocks(a):
            rest = a.shape[4:]
            return a.reshape(B, d, L, *rest).swapaxes(1, 2).reshape(B, Tp, *rest)

        qb = to_blocks(qp)
        kk = with_prev(to_blocks(kp))
        vv = with_prev(to_blocks(vp))
        bias = rel_bias[t5_bucket(d * np.clip(steps, 0, DIL_STEPS))]
        bias = jnp.transpose(bias, (2, 0, 1)).astype(jnp.float32)
        blk = np.arange(nb)[:, None, None]
        valid = band[None] & ((blk > 0) | (kj[None] >= DIL_STEPS))
        s = jnp.einsum('brnqhd,brnkhd->brnhqk', qb, kk,
                       preferred_element_type=jnp.float32) * scale + bias
        s = jnp.where(valid[None, None, :, None], s, -jnp.inf)
        m = jnp.max(s, axis=-1)
        e = jnp.exp(s - m[..., None])
        den = jnp.sum(e, axis=-1)
        o = jnp.einsum('brnhqk,brnkhd->brnqhd', e, vv.astype(jnp.float32))
        o = o / jnp.moveaxis(den, -1, -2)[..., None]
        outs.append(from_blocks(o)[:, :S])
        maxes.append(from_blocks(jnp.moveaxis(m, -1, -2))[:, :S])
        dens.append(from_blocks(jnp.moveaxis(den, -1, -2))[:, :S])
    return merge_dilations(outs, maxes, dens)

def dilated_attention_sample(q, k_new, v_new, cache_k, cache_v, rel_bias):
    S = q.shape[1]
    Lb = cache_k.shape[1]
    scale = HEAD_DIM ** -0.5
    j = np.arange(DIL_STEPS + 1)
    outs, maxes, dens = [], [], []
    for d in DILATIONS:
        idx = Lb + np.arange(S)[:, None] - d * j[None, :]
        valid = idx >= 0
        from_cache = (idx < Lb)[None, :, :, None, None]
        ci = np.clip(idx, 0, Lb - 1)
        ni = np.clip(idx - Lb, 0, S - 1)
        kg = jnp.where(from_cache, cache_k[:, ci], k_new[:, ni])
        vg = jnp.where(from_cache, cache_v[:, ci], v_new[:, ni])
        bias = rel_bias[t5_bucket(d * j)].T.astype(jnp.float32)
        s = jnp.einsum('bshd,bsjhd->bshj', q, kg,
                       preferred_element_type=jnp.float32) * scale + bias
        s = jnp.where(valid[None, :, None, :], s, -jnp.inf)
        m = jnp.max(s, axis=-1)
        e = jnp.exp(s - m[..., None])
        den = jnp.sum(e, axis=-1)
        o = jnp.einsum('bshj,bsjhd->bshd', e, vg.astype(jnp.float32)) / den[..., None]
        outs.append(o)
        maxes.append(m)
        dens.append(den)
    return merge_dilations(outs, maxes, dens)

def short_conv(u, buf, w):
    S = u.shape[1]
    up = jnp.concatenate([buf, u], axis=1)
    y = sum(w[t] * up[:, t:t + S] for t in range(CONV_W))
    return y, up[:, -(CONV_W - 1):]

def mix_inputs(x, g_mix, w_in, q_norm, k_norm):
    n = rms_norm(x, g_mix)
    proj = n @ w_in
    q, k, v, hc, bc, cc = jnp.split(proj, SPLITS, axis=-1)
    hs = x.shape[:2] + (N_HEADS, HEAD_DIM)
    q = rms_norm(q.reshape(hs), q_norm)
    k = rms_norm(k.reshape(hs), k_norm)
    v = v.reshape(hs)
    return q, k, v, cc * hc, bc

def mix_output(attn, conv, g_attn_out, g_conv_out, w_out):
    a = attn.reshape(attn.shape[:2] + (D_ATTN,))
    cat = jnp.concatenate([rms_norm(a, g_attn_out), rms_norm(conv, g_conv_out)], axis=-1)
    return cat @ w_out

def channel_and_ple(h, p, g_ffn, w_gate, w_up, w_down, g_ple, w_ple_gate, w_ple_proj):
    n = rms_norm(h, g_ffn)
    h = h + (jax.nn.silu(n @ w_gate) * (n @ w_up)) @ w_down
    gate = jax.nn.sigmoid(rms_norm(h, g_ple) @ w_ple_gate)
    return h + gate * (p @ w_ple_proj)

def setup_inputs(seed: int = 0) -> dict:
    key = jax.random.key(seed)
    ks = jax.random.split(key, 24)
    f32 = jnp.float32
    nrm = lambda k, shape, s=1.0: jax.random.normal(k, shape, f32) * s
    gain = lambda k, shape: 1.0 + 0.05 * jax.random.normal(k, shape, f32)
    L_buf = min(W_MAX, PAST_LEN)
    return {
        "x_prompt": nrm(ks[0], (BATCH, SEQ, D_MODEL)),
        "x_sample": nrm(ks[1], (DEC_BATCH, DEC_SEQ, D_MODEL)),
        "p_prompt": nrm(ks[2], (DEPTH, BATCH, SEQ, D_PLE)),
        "p_sample": nrm(ks[3], (DEPTH, DEC_BATCH, DEC_SEQ, D_PLE)),
        "cache_k": nrm(ks[4], (DEPTH, DEC_BATCH, L_buf, N_HEADS, HEAD_DIM)),
        "cache_v": nrm(ks[5], (DEPTH, DEC_BATCH, L_buf, N_HEADS, HEAD_DIM)),
        "state_conv": nrm(ks[6], (DEPTH, DEC_BATCH, CONV_W - 1, D_CONV)),
        "rel_bias": nrm(ks[7], (N_BUCKETS, N_HEADS), 0.5),
        "g_mix": gain(ks[8], (DEPTH, D_MODEL)),
        "w_in": nrm(ks[9], (DEPTH, D_MODEL, D_IN), D_MODEL ** -0.5),
        "q_norm": gain(ks[10], (DEPTH, HEAD_DIM)),
        "k_norm": gain(ks[11], (DEPTH, HEAD_DIM)),
        "conv_w": nrm(ks[12], (DEPTH, CONV_W, D_CONV), CONV_W ** -0.5),
        "g_attn_out": gain(ks[13], (DEPTH, D_ATTN)),
        "g_conv_out": gain(ks[14], (DEPTH, D_CONV)),
        "w_out": nrm(ks[15], (DEPTH, D_ATTN + D_CONV, D_MODEL), (D_ATTN + D_CONV) ** -0.5),
        "g_ffn": gain(ks[16], (DEPTH, D_MODEL)),
        "w_gate": nrm(ks[17], (DEPTH, D_MODEL, D_FF), D_MODEL ** -0.5),
        "w_up": nrm(ks[18], (DEPTH, D_MODEL, D_FF), D_MODEL ** -0.5),
        "w_down": nrm(ks[19], (DEPTH, D_FF, D_MODEL), D_FF ** -0.5),
        "g_ple": gain(ks[20], (DEPTH, D_MODEL)),
        "w_ple_gate": nrm(ks[21], (DEPTH, D_MODEL, D_MODEL), D_MODEL ** -0.5),
        "w_ple_proj": nrm(ks[22], (DEPTH, D_PLE, D_MODEL), D_PLE ** -0.5),
    }

def reference(x_prompt, x_sample, p_prompt, p_sample, cache_k, cache_v, state_conv,
              rel_bias, g_mix, w_in, q_norm, k_norm, conv_w, g_attn_out, g_conv_out, w_out,
              g_ffn, w_gate, w_up, w_down, g_ple, w_ple_gate, w_ple_proj):
    hp, hs = x_prompt, x_sample
    S = x_prompt.shape[1]
    kw = min(W_MAX, S)
    kp_l, vp_l, cp_l, ks_l, vs_l, cs_l = [], [], [], [], [], []
    for i in range(DEPTH):
        q, k, v, u, bc = mix_inputs(hp, g_mix[i], w_in[i], q_norm[i], k_norm[i])
        attn = dilated_attention_prompt(q, k, v, rel_bias).astype(hp.dtype)
        buf0 = jnp.zeros((hp.shape[0], CONV_W - 1, D_CONV), u.dtype)
        cy, c_new = short_conv(u, buf0, conv_w[i])
        hp = hp + mix_output(attn, bc * cy, g_attn_out[i], g_conv_out[i], w_out[i])
        hp = channel_and_ple(hp, p_prompt[i], g_ffn[i], w_gate[i], w_up[i], w_down[i],
                             g_ple[i], w_ple_gate[i], w_ple_proj[i])
        kp_l.append(k[:, S - kw:])
        vp_l.append(v[:, S - kw:])
        cp_l.append(c_new)
        q, k, v, u, bc = mix_inputs(hs, g_mix[i], w_in[i], q_norm[i], k_norm[i])
        attn = dilated_attention_sample(q, k, v, cache_k[i], cache_v[i], rel_bias).astype(hs.dtype)
        cy, c_new = short_conv(u, state_conv[i].astype(u.dtype), conv_w[i])
        hs = hs + mix_output(attn, bc * cy, g_attn_out[i], g_conv_out[i], w_out[i])
        hs = channel_and_ple(hs, p_sample[i], g_ffn[i], w_gate[i], w_up[i], w_down[i],
                             g_ple[i], w_ple_gate[i], w_ple_proj[i])
        ks_l.append(k)
        vs_l.append(v)
        cs_l.append(c_new)
    k_prompt = jnp.stack(kp_l)
    v_prompt = jnp.stack(vp_l)
    conv_prompt = jnp.stack(cp_l)
    k_sample = jnp.stack(ks_l)
    v_sample = jnp.stack(vs_l)
    conv_sample = jnp.stack(cs_l)
    return (hp, hs, k_prompt, v_prompt, conv_prompt, k_sample, v_sample, conv_sample)


_drawn_inputs = setup_inputs


def setup_inputs(seed=0):
    import zlib

    import numpy as np

    out = dict(_drawn_inputs(seed))
    spreads = {}
    factors = {'g_ple': 21.502}
    for name, (base, spread) in spreads.items():
        noise = np.random.default_rng([zlib.crc32(name.encode()), seed]).standard_normal(out[name].shape)
        drawn = base * np.exp(spread * noise) if base else spread * noise
        out[name] = __import__('jax').numpy.asarray(drawn.astype(out[name].dtype))
    for name, factor in factors.items():
        out[name] = (out[name] * factor).astype(out[name].dtype)
    return out
```

```python
from contextlib import ExitStack

import numpy as np

import concourse.bass as bass
from concourse import mybir

F32 = mybir.dt.float32
F32R = mybir.dt.float32r
ALU = mybir.AluOpType
ACT = mybir.ActivationFunctionType
X = mybir.AxisListType.X

P = 128
D_MODEL, SEQ, DEC, PAST = 2048, 512, 8, 256
HEADS, HD = 16, 64
D_ATTN = HEADS * HD
D_CONV = D_MODEL - D_ATTN
D_FF, D_PLE = 5632, 256
BUCKETS, MAX_EXACT, MAX_DIST = 32, 16, 2048
DIL_STEPS, DILATIONS = 128, (1, 4, 16)
EPS = 1e-6
MASKED = -1e30

T = SEQ + DEC
HALF = T // 2
KT = D_MODEL // P
KA = D_ATTN // P
KC = D_CONV // P
QB = SEQ // P
KU = 8
UNIT = KU * P
RAW, HILO = 2, 4
CHUNK = 11
CHUNKS = D_FF // P // CHUNK
DOWN = (6, 5)
KCACHE = PAST // P
KP = D_PLE // P
BIAS_W = 640
ROW_W = PAST + 1
V_, K_, Q_, H_, C_, B_ = 2 * D_ATTN, D_ATTN, 0, 3 * D_ATTN, 3 * D_ATTN + 2 * D_CONV, 3 * D_ATTN + D_CONV
KINDS = (V_, K_, Q_, H_, C_, B_)
PAIR_UNITS = 2 * len(KINDS)
U_CONV = KA * PAIR_UNITS
U_ATTN = U_CONV + KT
U_FFN = U_ATTN + KT
CHUNK_UNITS = 4 * CHUNK + 2 * KT
U_PLE = U_FFN + CHUNKS * CHUNK_UNITS
T_CONV = KA * len(KINDS)
T_ATTN = T_CONV + KT
T_FFN = T_ATTN + KT
CHUNK_TILES = 2 * CHUNK + KT
T_PLE = T_FFN + CHUNKS * CHUNK_TILES
ROWS = dict(mix=0, ffn=KT, ple=2 * KT, attn=3 * KT, conv=3 * KT + KA, taps=3 * KT + KA + KC)
ROWS["q"] = ROWS["taps"] + 3 * KC
ROWS["k"] = ROWS["q"] + 1
N_ROWS = ROWS["k"] + 1
SQ_CONV = 2 * (KC + KA - 1)
SQ_ATTN = 2 * (KC + KA)
SQ_FFN = SQ_ATTN + 2 * KT
SQ_PLE = SQ_FFN + 2 * KT
CONSTANTS = 13


def bucket_table():
    dist = SEQ - 1 - np.arange(BIAS_W)
    n = np.maximum(dist, 1)
    large = MAX_EXACT + (np.log(n.astype(np.float32) / MAX_EXACT)
                         / np.float32(np.log(MAX_DIST / MAX_EXACT)) * (BUCKETS - MAX_EXACT)).astype(np.int32)
    bucket = np.where(dist < MAX_EXACT, dist, np.minimum(large, BUCKETS - 1))
    count = sum(((dist >= 0) & (dist % d == 0) & (dist <= d * DIL_STEPS)).astype(int) for d in DILATIONS)
    table = np.zeros((BUCKETS + 1, BIAS_W), np.float32)
    for x in range(BIAS_W):
        if count[x]:
            table[bucket[x], x] = 1.0
            table[BUCKETS, x] = np.log(float(count[x]))
        else:
            table[BUCKETS, x] = MASKED
    return table


class Span:

    def __init__(self, first, per=0, turn=0):
        assert first % HILO == 0 and per % HILO == 0
        self.first, self.per, self.turn = first, per, turn

    def count(self, u):
        return self.turn * self.per + (self.first + u + 1)

    def landed(self, u):
        return self.turn * (16 * self.per // RAW) + 16 * ((self.first + u) // RAW + 1)


def build(nc, x_prompt, x_sample, p_prompt, p_sample, cache_k, cache_v, state_conv, rel_bias, g_mix,
          w_in, q_norm, k_norm, conv_w, g_attn_out, g_conv_out, w_out, g_ffn, w_gate, w_up, w_down,
          g_ple, w_ple_gate, w_ple_proj, table,
          y_prompt, y_sample, k_prompt, v_prompt, conv_prompt, k_sample, v_sample, conv_sample):
    w_in, w_out, w_gate, w_up, w_down = w_in[0], w_out[0], w_gate[0], w_up[0], w_down[0]
    w_ple_gate, w_ple_proj = w_ple_gate[0], w_ple_proj[0]

    xt_dram = nc.dram_tensor("xt_dram", (P, KT, T), F32, kind="Internal").ap()
    bias_dram = nc.dram_tensor("bias_dram", (HEADS, BIAS_W), F32, kind="Internal").ap()
    skew_dram = nc.dram_tensor("skew_dram", (HEADS, P, SEQ), F32, kind="Internal").ap()
    row_dram = nc.dram_tensor("row_dram", (KA, DEC, 2, ROW_W), F32, kind="Internal").ap()

    ctx = ExitStack()

    def sem(name):
        return ctx.enter_context(nc.semaphore(name))

    def sb(name, shape, dt=F32, scope=None):
        return (scope or ctx).enter_context(nc.sbuf_tensor(name, shape, dt))

    wraw = sb("wraw", [P, RAW, UNIT])
    whi = sb("whi", [P, HILO, UNIT], F32R)
    wlo = sb("wlo", [P, HILO, UNIT], F32R)
    xhi = sb("xhi", [P, KT, T], F32R)
    xlo = sb("xlo", [P, KT, T], F32R)
    hid = sb("hid", [P, KT, T])
    cols = sb("cols", [P, N_ROWS])
    ident = sb("ident", [P, P])
    ones = sb("ones", [P, P])
    rstd = sb("rstd", [P, T])
    acc_conv = sb("acc_conv", [P, T])
    acc_attn = sb("acc_attn", [P, T])
    gsq = sb("gsq", [P, T])
    tmp = sb("tmp", [P, 4, T])
    headsum = sb("headsum", [P, P])
    half_mask = sb("half_mask", [P, 2])
    state_t = sb("state_t", [P, KC, 2 * DEC])
    qdiag = tmp[:, 3, 0:4 * P].rearrange("p (b f) -> p b f", b=4)
    row = tmp[0:2 * DEC, 3, 0:ROW_W]
    conv, gate_t, sq, qk_rstd = (tmp[:, n, :] for n in range(4))
    res, act_t, rstd_attn = tmp[:, 0:2, :], tmp[:, 2, :], tmp[:, 3, :]

    mix = ExitStack()
    v_t = sb("v_t", [P, T], scope=mix)
    k_t = sb("k_t", [P, T], scope=mix)
    q_t = sb("q_t", [P, T], scope=mix)
    khi = sb("khi", [P, SEQ], F32R, mix)
    klo = sb("klo", [P, SEQ], F32R, mix)
    qhi = sb("qhi", [P, SEQ], F32R, mix)
    qlo = sb("qlo", [P, SEQ], F32R, mix)
    v_nat = sb("v_nat", [P, QB, P], scope=mix)
    k_nat = sb("k_nat", [P, QB, P], scope=mix)
    vhi = sb("vhi", [P, QB, P], F32R, mix)
    vlo = sb("vlo", [P, QB, P], F32R, mix)
    small_nat = sb("small_nat", [DEC + 2, 3, P], scope=mix)
    u_t = sb("u_t", [P, 2 + T], scope=mix)
    skew = sb("skew", [P, 2, SEQ], scope=mix)
    prob = sb("prob", [P, 2, SEQ], scope=mix)
    pthi = sb("pthi", [P, 2, SEQ], F32R, mix)
    ptlo = sb("ptlo", [P, 2, SEQ], F32R, mix)
    stats = sb("stats", [P, 4], scope=mix)
    kv = sb("kv", [P, DEC * KCACHE, P], scope=mix)
    qkv_s = sb("qkv_s", [P, 3, DEC], scope=mix)
    kq_s = sb("kq_s", [P, DEC], scope=mix)
    kq_pair = sb("kq_pair", [P, DEC, 2], scope=mix)
    key_sc = sb("key_sc", [P, KCACHE, 2 * DEC], scope=mix)
    row_bias = sb("row_bias", [2 * DEC, ROW_W], scope=mix)
    row_stats = sb("row_stats", [2 * DEC, 4], scope=mix)
    new_diag = sb("new_diag", [2 * DEC, 2 * DEC], scope=mix)
    p_cols = sb("p_cols", [P, 3, 2 * DEC], scope=mix)
    out_s = sb("out_s", [P, DEC, 2], scope=mix)
    mix.close()

    start = ExitStack()
    x_nat = sb("x_nat", [P, QB, D_MODEL], scope=start)
    xs_nat = sb("xs_nat", [DEC, D_MODEL], scope=start)
    gain_rows = sb("gain_rows", [N_ROWS, P], scope=start)
    state_nat = sb("state_nat", [2 * DEC, D_CONV], scope=start)
    rel = sb("rel", [BUCKETS + 1, HEADS], scope=start)
    table_sb = sb("table_sb", [BUCKETS + 1, BIAS_W], scope=start)
    bias_sb = sb("bias_sb", [HEADS, BIAS_W], scope=start)
    x_sum = sb("x_sum", [P, QB + 1], scope=start)
    x_rs = sb("x_rs", [P, QB + 1], scope=start)
    xdiag = sb("xdiag", [P, QB, P], scope=start)
    xsdiag = sb("xsdiag", [DEC, DEC], scope=start)
    start.close()

    ffn = ExitStack()
    p_nat = sb("p_nat", [P, QB, D_PLE], scope=ffn)
    ps_nat = sb("ps_nat", [DEC, D_PLE], scope=ffn)
    hidden = ExitStack()
    fhi = sb("fhi", [P, CHUNK, T], F32R, hidden)
    flo = sb("flo", [P, CHUNK, T], F32R, hidden)
    hidden.close()
    phi = sb("phi", [P, KP, T], F32R, ffn)
    plo = sb("plo", [P, KP, T], F32R, ffn)
    y_t = sb("y_t", [P, T], scope=ffn)
    y_nat = sb("y_nat", [P, 2, QB, P], scope=ffn)
    ys_nat = sb("ys_nat", [DEC, 2, P], scope=ffn)
    ffn.close()

    acc = ctx.enter_context(nc.psum_tensor("acc", [P, 2, 2, 512], F32))
    aux = ctx.enter_context(nc.psum_tensor("aux", [P, 4, 512], F32))
    BANK_S, BANK_D, BANK_T, BANK_O = range(4)

    def halves(tile):
        return tile.rearrange("p (h t) -> p h t", h=2)

    def acc_of(slot):
        return acc[:, slot, :, 0:HALF]

    aux_sum = aux[:, BANK_S:BANK_D + 1, 0:HALF]

    landed = [sem(f"unit_landed{i}") for i in range(RAW)]
    s_whi = sem("weights_hi_written")
    s_wlo = sem("weights_split")
    s_unit = sem("unit_multiplied")
    s_read = sem("product_read")
    s_x = sem("operand_tile_split")
    s_xhi = sem("operand_hi_written")
    l_rows, l_xs, l_table, l_state = sem("rows_landed"), sem("xs_landed"), sem("table_landed"), sem("state_landed")
    l_x = [sem(f"x_landed{g}") for g in range(4)]
    s_const, s_tr0, s_cp0, s_xt = sem("constants"), sem("start_transposed"), sem("start_copied"), sem("xt_copied")
    s_sum, s_xrs, s_xrstd, s_xdiag = sem("x_summed"), sem("x_root"), sem("x_rstd"), sem("x_diagonals")
    s_rsb, s_rstd = sem("rstd_spread"), sem("rstd_ready")
    s_bias, d_bias, d_skew, d_rows, d_spill = (sem("bias_rows"), sem("bias_stored"), sem("skew_stored"),
                                               sem("row_bias_stored"), sem("xt_stored"))
    d_state = sem("old_state_passed_on")
    s_sq, s_ssq, s_root, s_inv = sem("squared"), sem("heads_summed"), sem("root_ready"), sem("inverse_ready")
    s_qk, s_cols = sem("qk_normed"), sem("sample_cols")
    s_qkhi, s_qk2 = sem("qk_hi"), sem("qk_split")
    s_nat, s_natsb, s_vhi, s_v2 = sem("nat_transposed"), sem("nat_copied"), sem("v_hi"), sem("v_split")
    s_u, s_tap, s_conv = sem("u_ready"), sem("conv_tap"), sem("conv_ready")
    s_ident, s_sqs, s_zero = sem("identity_cleared"), sem("squares_step"), sem("squares_cleared")
    d_v, d_k, d_small = sem("v_stored"), sem("k_stored"), sem("small_stored")
    l_skew = sem("skew_landed")
    s_score, s_biased, s_max, s_nmax, s_exp = (sem("scores"), sem("biased"), sem("row_max"), sem("row_max_negated"),
                                               sem("exponentials"))
    s_rden, s_prob, s_pt, s_pthi, s_pt2, s_pv, s_o = (sem("row_sum_inverted"), sem("probabilities"),
                                                      sem("probs_transposed"), sem("probs_hi"), sem("probs_split"),
                                                      sem("values_weighted"), sem("attention_read"))
    l_kc, l_vc, l_row = sem("cached_k_landed"), sem("cached_v_landed"), sem("row_bias_landed")
    s_qd, s_qb, s_mul, s_key, s_str, s_row, s_sexp, s_pc, s_spv, s_out = (
        sem("q_diagonal"), sem("q_spread"), sem("keys_times_q"), sem("key_scores"), sem("samples_transposed"),
        sem("row_step"), sem("row_exponentials"), sem("prob_columns"), sem("cached_values_weighted"),
        sem("sample_step"))
    s_nsum, s_nroot, s_ninv = sem("norm_summed"), sem("norm_root"), sem("norm_rstd")
    l_res = [sem(f"residual_landed{i}") for i in range(2)]
    s_h = sem("h_tile_summed")
    s_sig, s_f, s_fhi, s_f2 = sem("sigmoid"), sem("hidden_step"), sem("hidden_hi"), sem("hidden_split")
    l_p, s_ptr, s_phi, s_p2 = sem("p_landed"), sem("p_transposed"), sem("p_hi"), sem("p_split")
    s_y, s_ytr, s_ycp = sem("y_step"), sem("y_transposed"), sem("y_copied")
    d_y = [sem(f"y_stored{i}") for i in range(2)]

    s_freed, s_passed = sem("sync_waits_passed"), sem("pool_waits_passed")

    FIRST = Span(0)
    block = ctx.enter_context(nc.Block())

    @block.sync
    def _(sp):
        def load(at, u, w, k0, nk, col):
            if not (at.first + u < RAW):
                sp.wait_ge(s_wlo, at.count(u) - RAW)
                sp.sem_inc(s_freed, 1)
            sp.dma_start(wraw[:, u % RAW, 0:nk * P].rearrange("p (k m) -> p k m", k=nk),
                         w[k0 * P:(k0 + nk) * P, bass.ds(col, P)].rearrange("(k p) m -> p k m", p=P)
                         ).then_inc(landed[u % RAW], 16)

        def pair(at, j):
            for n, kind in enumerate(KINDS):
                load(at, 2 * n, w_in, 0, KU, j * P + kind)
                load(at, 2 * n + 1, w_in, KU, KU, j * P + kind)

        pair(FIRST, 0)
        with sp.Fori(0, KA - 1) as a:
            pair(Span(PAIR_UNITS, PAIR_UNITS, a), a + 1)
        for first, k0 in ((U_CONV, KA), (U_ATTN, 0)):
            for part, m0 in enumerate((KT // 2, 0)):
                with sp.Fori(0, 2) as i:
                    at = Span(first + part * KT // 2, 4, i)
                    for b in range(4):
                        load(at, b, w_out, k0, KU, i * (4 * P) + (m0 + b) * P)

        def chunk_of(first, row0, col0):
            with sp.Fori(0, CHUNK) as f:
                at = Span(first, 4, f)
                for n, w in enumerate((w_gate, w_up)):
                    load(at, 2 * n, w, KU, KU, f * P + col0)
                    load(at, 2 * n + 1, w, 0, KU, f * P + col0)
            with sp.Fori(0, KT // 2) as i:
                at = Span(first + 4 * CHUNK, 4, i)
                for b in range(2):
                    load(at, 2 * b, w_down, row0, DOWN[0], i * (2 * P) + b * P)
                    load(at, 2 * b + 1, w_down, row0 + DOWN[0], DOWN[1], i * (2 * P) + b * P)

        for c in range(CHUNKS):
            chunk_of(U_FFN + c * CHUNK_UNITS, c * CHUNK, c * CHUNK * P)
        with sp.Fori(0, KT // 4) as i:
            at = Span(U_PLE, 12, i)
            for b in range(4):
                load(at, 3 * b, w_ple_gate, KU, KU, i * (4 * P) + b * P)
                load(at, 3 * b + 1, w_ple_gate, 0, KU, i * (4 * P) + b * P)
                load(at, 3 * b + 2, w_ple_proj, 0, KP, i * (4 * P) + b * P)

    @block.tensor
    def _(pe):
        mm = nc.tensor.matmul

        def unit(at, u, hi, lo, tiles, slot, first, last, ready=None):
            pe.wait_ge(s_wlo, at.count(u))
            for n, kt in enumerate(tiles):
                if ready:
                    pe.wait_ge(ready[0], ready[1] + n)
                w_h = whi[:, u % HILO, n * P:(n + 1) * P]
                w_l = wlo[:, u % HILO, n * P:(n + 1) * P]
                begin, end = first and n == 0, last and n == len(tiles) - 1
                for h in range(2):
                    mm(acc[:, slot, h, 0:HALF], w_h, hi[:, kt, h * HALF:(h + 1) * HALF], start=begin, stop=False)
                for h in range(2):
                    mm(acc[:, slot, h, 0:HALF], w_h, lo[:, kt, h * HALF:(h + 1) * HALF], start=False, stop=False)
                for h in range(2):
                    done = mm(acc[:, slot, h, 0:HALF], w_l, hi[:, kt, h * HALF:(h + 1) * HALF], start=False, stop=end)
            done.then_inc(s_unit, 1)

        def spread_sum(lhs, tile):
            for h in range(2):
                done = mm(aux[:, BANK_S + h, 0:HALF], lhs[:, :], tile[:, h * HALF:(h + 1) * HALF], start=True, stop=True)
            return done

        def products(out, hi, lo, rhi, rlo, begin, end):
            mm(out, hi, rhi, start=begin, stop=False)
            mm(out, hi, rlo, start=False, stop=False)
            return mm(out, lo, rhi, start=False, stop=end)

        def attention(a, g):
            if 1 <= g <= 8:
                c = g - 1
                if c == 0:
                    pe.wait_ge(s_natsb, 5 * a + 5)
                else:
                    pe.wait_ge(s_pt2, 8 * a + c)
                pe.wait_ge(s_prob, 8 * a + (c + 1))
                for kb in range(c % QB + 1):
                    done = nc.tensor.transpose(aux[:, BANK_T, kb * P:(kb + 1) * P],
                                               prob[:, c % 2, kb * P:(kb + 1) * P], ident[:, :])
                done.then_inc(s_pt, 1)
            if 2 <= g <= 9:
                c = g - 2
                qb = c % QB
                if c == 0:
                    pe.wait_ge(s_v2, a + 1)
                if c == QB:
                    pe.wait_ge(s_o, 2 * a + 1)
                pe.wait_ge(s_pt2, 8 * a + (c + 1))
                for kb in range(qb + 1):
                    done = products(aux[:, BANK_O, qb * P:(qb + 1) * P], vhi[:, kb, :], vlo[:, kb, :],
                                    pthi[:, c % 2, kb * P:(kb + 1) * P], ptlo[:, c % 2, kb * P:(kb + 1) * P],
                                    kb == 0, kb == qb)
                done.then_inc(s_pv, 1)
            if g <= 7:
                e, qb = g // QB, g % QB
                if g == 0:
                    pe.wait_ge(s_root, 2 * a + 2)
                    pe.wait_ge(s_qk2, 2 * a + 2)
                else:
                    pe.wait_ge(s_biased, 8 * a + g)
                rows = slice(e * HD, (e + 1) * HD)
                done = products(aux[:, BANK_S, 0:(qb + 1) * P],
                                qhi[rows, qb * P:(qb + 1) * P], qlo[rows, qb * P:(qb + 1) * P],
                                khi[rows, 0:(qb + 1) * P], klo[rows, 0:(qb + 1) * P], True, True)
                done.then_inc(s_score, 1)
            if g in (1, 2):
                if g == 2:
                    pe.wait_ge(s_mul, 2 * a + 1)
                pe.wait_ge(s_qd, 2 * a + g)
                mm(aux[:, BANK_D, :], ones[:, :], qdiag[:, :, :], start=True, stop=True).then_inc(s_qb, 1)
            if g == 3:
                pe.wait_ge(s_key, 4 * a + 4)
                for t in range(KCACHE):
                    nc.tensor.transpose(aux[0:2 * DEC, BANK_D, t * P:(t + 1) * P], key_sc[:, t, :], ident[:, :])
                mm(aux[0:2 * DEC, BANK_D, PAST:PAST + 1], kq_pair[:, :, :], ones[:, 0:1],
                   start=True, stop=True).then_inc(s_str, 1)
            if g == 5:
                pe.wait_ge(s_row, 6 * a + 6)
                mm(aux[:, BANK_D, KCACHE * 2 * DEC:(KCACHE + 1) * 2 * DEC], ones[0:2 * DEC, :], new_diag[:, :],
                   start=True, stop=True)
                for t in range(KCACHE):
                    done = nc.tensor.transpose(aux[:, BANK_D, t * 2 * DEC:(t + 1) * 2 * DEC],
                                               row[:, t * P:(t + 1) * P], ident[0:2 * DEC, 0:2 * DEC])
                done.then_inc(s_str, 1)
            if g == 6:
                pe.wait_ge(s_pc, a + 1)
                pe.wait_ge(l_vc, 16 * a + 16)
                for b in range(DEC):
                    for t in range(KCACHE):
                        done = mm(aux[:, BANK_D, 2 * b:2 * b + 2], kv[:, KCACHE * b + t, :],
                                  p_cols[:, t, 2 * b:2 * b + 2], start=t == 0, stop=t == KCACHE - 1)
                done.then_inc(s_spv, 1)

        def heads(j, a, g):
            if g == 9:
                if a is not None:
                    pe.wait_ge(s_biased, 8 * a + 8)
                    pe.wait_ge(s_out, 4 * a + 4)
                pe.wait_ge(s_sq, 2 * j + 1)
                spread_sum(headsum, sq).then_inc(s_ssq, 1)
            if g == 10:
                pe.wait_ge(s_root, 2 * j + 1)
                pe.wait_ge(s_sq, 2 * j + 2)
                spread_sum(headsum, sq).then_inc(s_ssq, 1)
                if a is not None:
                    pe.wait_ge(s_pt2, 8 * a + 8)
                    pe.wait_ge(s_o, 2 * a + 2)
                pe.wait_ge(s_read, 6 * j + 1)
                nc.tensor.transpose(aux[0:DEC, BANK_O, 0:P], v_t[:, SEQ:T], ident[:, :])
                for b in range(QB):
                    done = nc.tensor.transpose(aux[:, BANK_T, b * P:(b + 1) * P], v_t[:, b * P:(b + 1) * P], ident[:, :])
                done.then_inc(s_nat, 1)
            if g == 11:
                pe.wait_ge(s_natsb, 5 * j + 2)
                pe.wait_ge(s_qk, 2 * j + 1)
                pe.wait_ge(s_u, j + 1)
                nc.tensor.transpose(aux[0:DEC, BANK_O, P:2 * P], k_t[:, SEQ:T], ident[:, :])
                nc.tensor.transpose(aux[0:DEC + 2, BANK_O, 2 * P:3 * P], u_t[:, SEQ:SEQ + 2 + DEC], ident[:, :])
                for b in range(QB):
                    done = nc.tensor.transpose(aux[:, BANK_T, b * P:(b + 1) * P], k_t[:, b * P:(b + 1) * P], ident[:, :])
                done.then_inc(s_nat, 1)

        def pair(at, j, a):
            for g in range(PAIR_UNITS):
                n = g // 2
                if g % 2 == 0 and (a is not None or n >= 2):
                    pe.wait_ge(s_read, 6 * j + (n - 1))
                unit(at, g, xhi, xlo, range(g % 2 * KU, (g % 2 + 1) * KU), n % 2, g % 2 == 0, g % 2 == 1,
                     (s_x, g * KU + 1) if a is None and g < 2 else None)
                if a is None and g == 2:
                    pe.wait_ge(s_xdiag, 2)
                    mm(aux[:, BANK_S, :], ones[:, :], xdiag[:, :, :], start=True, stop=True)
                    mm(aux[:, BANK_D, 0:DEC], ones[0:DEC, :], xsdiag[:, :], start=True, stop=True).then_inc(s_rsb, 1)
                if a is not None:
                    attention(a, g)
                heads(j, a, g)

        pe.wait_ge(s_const, CONSTANTS)
        pe.wait_ge(l_rows, 16 * 10)
        nc.tensor.transpose(acc[:, 1, 1, 0:N_ROWS], gain_rows[:, :], ident[0:N_ROWS, 0:N_ROWS]).then_inc(s_tr0, 1)
        pe.wait_ge(l_xs, 16)
        for t in range(KT):
            done = nc.tensor.transpose(acc[:, 1, 0, t * DEC:(t + 1) * DEC], xs_nat[:, t * P:(t + 1) * P],
                                       ident[0:DEC, 0:DEC])
        done.then_inc(s_tr0, 1)
        for t in range(KT):
            if t % 4 == 0:
                pe.wait_ge(l_x[t // 4], 16)
            if t >= 4:
                pe.wait_ge(s_xt, t - 3)
            for b in range(QB):
                done = nc.tensor.transpose(aux[:, t % 4, b * P:(b + 1) * P], x_nat[:, b, t * P:(t + 1) * P], ident[:, :])
            done.then_inc(s_tr0, 1)
        pe.wait_ge(l_state, 16)
        for t in range(KC):
            done = nc.tensor.transpose(acc[:, 0, 0, t * 2 * DEC:(t + 1) * 2 * DEC], state_nat[:, t * P:(t + 1) * P],
                                       ident[0:2 * DEC, 0:2 * DEC])
        pe.wait_ge(l_table, 32)
        pe.wait_ge(s_cp0, 2)
        for h in range(2):
            done = mm(acc[0:HEADS, 1, h, 0:BIAS_W // 2], rel[:, :], table_sb[:, h * BIAS_W // 2:(h + 1) * BIAS_W // 2],
                      start=True, stop=True)
        done.then_inc(s_tr0, 1)
        pe.wait_ge(s_xt, KT)
        pe.wait_ge(s_cp0, 4)

        pair(FIRST, 0, None)
        with pe.Fori(0, KA - 1) as a:
            pair(Span(PAIR_UNITS, PAIR_UNITS, a), a + 1, a)

        at = Span(U_CONV)
        for i in range(KT):
            pe.wait_ge(s_read, T_CONV + i - 1)
            unit(at, i, xhi, xlo, range(KA, KT), i % 2, True, True, (s_x, KT + 1) if i == 0 else None)
            if i == 0:
                pe.wait_ge(s_sqs, SQ_CONV)
                pe.wait_ge(s_root, 2 * KA)
                pe.wait_ge(s_natsb, 5 * KA)
                mm(aux[:, BANK_D, 0:HALF], ones[:, :], acc_conv[:, 0:HALF], start=True, stop=True)
                mm(aux[:, BANK_O, 0:HALF], ones[:, :], acc_conv[:, HALF:T], start=True, stop=True).then_inc(s_nsum, 1)
            if i == 1:
                pe.wait_ge(s_nroot, 1)
            if i < PAIR_UNITS:
                attention(KA - 1, i)
            if i == 13:
                pe.wait_ge(s_sqs, SQ_ATTN)
                spread_sum(ones, acc_attn).then_inc(s_nsum, 1)

        with pe.Fori(0, 4) as i:
            at = Span(U_ATTN, 4, i)
            for b in range(4):
                pe.wait_ge(s_read, i * 4 + (T_ATTN + b - 1))
                unit(at, b, xhi, xlo, range(KA), b % 2, True, True, (s_x, KT + KC + 1) if b == 0 else None)

        def f_tile(at, c, f, fresh=False):
            for n in range(2):
                pe.wait_ge(s_read, f * 2 + (T_FFN + c * CHUNK_TILES + n - 1))
                for part, k0 in enumerate((KU, 0)):
                    unit(at, 2 * n + part, xhi, xlo, range(k0, k0 + KU), n, part == 0, part == 1,
                         (s_x, 2 * KT + 1 + part * KU) if fresh and n == 0 else None)
                if fresh and n == 0:
                    pe.wait_ge(s_sqs, SQ_FFN)
                    spread_sum(ones, acc_attn).then_inc(s_nsum, 1)

        for c in range(CHUNKS):
            first = U_FFN + c * CHUNK_UNITS
            if c == 0:
                f_tile(Span(first), 0, 0, fresh=True)
                with pe.Fori(0, CHUNK - 1) as f:
                    f_tile(Span(first + 4, 4, f), c, f + 1)
            else:
                with pe.Fori(0, CHUNK) as f:
                    f_tile(Span(first, 4, f), c, f)
            with pe.Fori(0, KT // 2) as i:
                at = Span(first + 4 * CHUNK, 4, i)
                for b in range(2):
                    pe.wait_ge(s_read, i * 2 + (T_FFN + c * CHUNK_TILES + 2 * CHUNK + b - 1))
                    pe.wait_ge(s_f2, c * CHUNK + DOWN[0])
                    unit(at, 2 * b, fhi, flo, range(DOWN[0]), b, True, False)
                    pe.wait_ge(s_f2, (c + 1) * CHUNK)
                    unit(at, 2 * b + 1, fhi, flo, range(DOWN[0], CHUNK), b, False, True)

        def transpose_y(n):
            pe.wait_ge(s_y, n)
            nc.tensor.transpose(aux[0:DEC, BANK_D, 0:P], y_t[:, SEQ:T], ident[:, :])
            for b in range(QB):
                done = nc.tensor.transpose(aux[:, BANK_S, b * P:(b + 1) * P], y_t[:, b * P:(b + 1) * P], ident[:, :])
            done.then_inc(s_ytr, 1)

        def embed(i, first_turn):
            at = Span(U_PLE, 12, i)
            for b in range(4):
                m = i * 4 + b
                pe.wait_ge(s_read, m * 2 + (T_PLE - 1))
                fresh = first_turn and b == 0
                unit(at, 3 * b, xhi, xlo, range(KU, KT), 0, True, False, (s_x, 3 * KT + KU + 1) if fresh else None)
                if fresh:
                    pe.wait_ge(l_p, 32)
                    for t in range(KP):
                        for q in range(QB):
                            nc.tensor.transpose(aux[:, BANK_T + t, q * P:(q + 1) * P], p_nat[:, q, t * P:(t + 1) * P],
                                                ident[:, :])
                    for t in range(KP):
                        done = nc.tensor.transpose(aux[:, BANK_D, t * DEC:(t + 1) * DEC],
                                                   ps_nat[:, t * P:(t + 1) * P], ident[0:DEC, 0:DEC])
                    done.then_inc(s_ptr, 1)
                else:
                    if first_turn and b == 1:
                        pe.wait_ge(s_nroot, 4)
                    else:
                        pe.wait_ge(s_ycp, (m - 1) * 2)
                    transpose_y(m)
                unit(at, 3 * b + 1, xhi, xlo, range(KU), 0, False, True)
                if fresh:
                    pe.wait_ge(s_sqs, SQ_PLE)
                    pe.wait_ge(s_p2, KP)
                    spread_sum(ones, acc_attn).then_inc(s_nsum, 1)
                pe.wait_ge(s_read, m * 2 + T_PLE)
                unit(at, 3 * b + 2, phi, plo, range(KP), 1, True, True)

        embed(0, True)
        with pe.Fori(1, KT // 4) as i:
            embed(i, False)
        pe.wait_ge(s_ycp, (KT - 1) * 2)
        transpose_y(KT)

    @block.scalar
    def _(act):
        on = nc.scalar.activation

        def split(at, u):
            act.wait_ge(landed[u % RAW], at.landed(u))
            if not (at.first + u < HILO):
                act.wait_ge(s_unit, at.count(u) - HILO)
            on(whi[:, u % HILO, :], wraw[:, u % RAW, :], ACT.Copy).then_inc(s_whi, 1)

        def split_short(at, u, nk):
            act.wait_ge(landed[u % RAW], at.landed(u))
            act.wait_ge(s_unit, at.count(u) - HILO)
            on(whi[:, u % HILO, 0:nk * P], wraw[:, u % RAW, 0:nk * P], ACT.Copy).then_inc(s_whi, 1)

        def root_of(tile, width):
            return on(halves(tile[:, :]), aux_sum, ACT.Sqrt, bias=EPS, scale=1.0 / width)

        def attention(a, g):
            if 1 <= g <= 8:
                c = g - 1
                w = (c % QB + 1) * P
                act.wait_ge(s_pt, 8 * a + (c + 1))
                if c >= 2:
                    act.wait_ge(s_pv, 8 * a + (c - 1))
                on(pthi[:, c % 2, 0:w], aux[:, BANK_T, 0:w], ACT.Copy).then_inc(s_pthi, 1)
            if g <= 7:
                w = (g % QB + 1) * P
                act.wait_ge(s_nmax, 8 * a + (g + 1))
                on(prob[:, g % 2, 0:w], prob[:, g % 2, 0:w], ACT.Exp, bias=stats[:, 1:2],
                   accum_out=stats[:, 2:3]).then_inc(s_exp, 1)
            if g == 3:
                act.wait_ge(s_row, 6 * a + 3)
                on(row[:, :], row[:, :], ACT.Exp, bias=row_stats[:, 1:2], accum_out=row_stats[:, 2:3]
                   ).then_inc(s_sexp, 1)

        def heads(j, a, g):
            if g == 7:
                if a is not None:
                    act.wait_ge(s_ssq, 2 * j)
                act.wait_ge(s_read, 6 * j + 2)
                on(sq[:, :], k_t[:, :], ACT.Square).then_inc(s_sq, 1)
            if g == 9:
                act.wait_ge(s_ssq, 2 * j + 1)
                if a is not None:
                    act.wait_ge(s_qk, 2 * j)
                root_of(qk_rstd, HD).then_inc(s_root, 1)
                act.wait_ge(s_read, 6 * j + 3)
                on(sq[:, :], q_t[:, :], ACT.Square).then_inc(s_sq, 1)
                act.wait_ge(s_qk, 2 * j + 1)
                if a is not None:
                    act.wait_ge(s_score, 8 * a + 8)
                on(khi[:, :], k_t[:, 0:SEQ], ACT.Copy).then_inc(s_qkhi, 1)
            if g == 10:
                act.wait_ge(s_ssq, 2 * j + 2)
                root_of(qk_rstd, HD).then_inc(s_root, 1)
                act.wait_ge(s_nat, 2 * j + 1)
                if a is not None:
                    act.wait_ge(d_v, 16 * j)
                    act.wait_ge(d_small, 64 * j)
                on(v_nat[:, :, :], aux[:, BANK_T, :].rearrange("p (b f) -> p b f", b=QB), ACT.Copy).then_inc(s_natsb, 1)
                on(small_nat[0:DEC, 0, :], aux[0:DEC, BANK_O, 0:P], ACT.Copy).then_inc(s_natsb, 1)
                if a is not None:
                    act.wait_ge(s_pv, 8 * a + 8)
                act.wait_ge(s_natsb, 5 * j + 1)
                on(vhi[:, :, :], v_nat[:, :, :], ACT.Copy).then_inc(s_vhi, 1)
                act.wait_ge(s_qk, 2 * j + 2)
                on(qhi[:, :], q_t[:, 0:SEQ], ACT.Copy).then_inc(s_qkhi, 1)
            if g == 11:
                act.wait_ge(s_nat, 2 * j + 2)
                if a is not None:
                    act.wait_ge(d_k, 16 * j)
                on(k_nat[:, :, :], aux[:, BANK_T, :].rearrange("p (b f) -> p b f", b=QB), ACT.Copy).then_inc(s_natsb, 1)
                on(small_nat[0:DEC, 1, :], aux[0:DEC, BANK_O, P:2 * P], ACT.Copy).then_inc(s_natsb, 1)
                on(small_nat[0:DEC + 2, 2, :], aux[0:DEC + 2, BANK_O, 2 * P:3 * P], ACT.Copy).then_inc(s_natsb, 1)

        def pair(at, j, a):
            for g in range(PAIR_UNITS):
                split(at, g + HILO)
                if a is not None:
                    attention(a, g)
                heads(j, a, g)

        def operand_hi(m, source, gain):
            return on(xhi[:, m, :], source, ACT.Copy, scale=cols[:, bass.ds(m + gain, 1)])

        for g in range(4):
            act.dma_start(x_nat[:, :, g * 512:(g + 1) * 512],
                          x_prompt[0, :, g * 512:(g + 1) * 512].rearrange("(b p) f -> p b f", p=P)
                          ).then_inc(l_x[g], 16)
        act.wait_ge(s_tr0, 1)
        on(cols[:, :], acc[:, 1, 1, 0:N_ROWS], ACT.Copy).then_inc(s_cp0, 1)
        act.wait_ge(s_tr0, 2)
        on(hid[:, :, SEQ:T], acc[:, 1, 0, 0:KT * DEC].rearrange("p (t b) -> p t b", b=DEC), ACT.Copy).then_inc(s_cp0, 1)
        for t in range(KT):
            act.wait_ge(s_tr0, t + 3)
            on(hid[:, t, 0:SEQ], aux[:, t % 4, :], ACT.Copy).then_inc(s_xt, 1)
            if t == 3:
                split(FIRST, 0)
            if t == 9:
                split(FIRST, 1)
        act.wait_ge(s_tr0, KT + 3)
        on(state_t[:, :, :], acc[:, 0, 0, 0:KC * 2 * DEC].rearrange("p (t b) -> p t b", t=KC), ACT.Copy).then_inc(s_cp0, 1)
        on(bias_sb.rearrange("h (a w) -> h a w", a=2), acc[0:HEADS, 1, :, 0:BIAS_W // 2], ACT.Copy).then_inc(s_cp0, 1)
        for b in range(QB):
            on(x_nat[:, b, :], x_nat[:, b, :], ACT.Square, accum_out=x_sum[:, b:b + 1]).then_inc(s_sum, 1)
        on(xs_nat[:, :], xs_nat[:, :], ACT.Square, accum_out=x_sum[0:DEC, QB:QB + 1]).then_inc(s_sum, 1)
        act.wait_ge(s_sum, QB + 1)
        on(x_rs[:, 0:QB], x_sum[:, 0:QB], ACT.Sqrt, bias=EPS, scale=1.0 / D_MODEL).then_inc(s_xrs, 1)
        on(x_rs[0:DEC, QB:QB + 1], x_sum[0:DEC, QB:QB + 1], ACT.Sqrt, bias=EPS, scale=1.0 / D_MODEL).then_inc(s_xrs, 1)
        split(FIRST, 2)
        split(FIRST, 3)

        pair(FIRST, 0, None)
        with act.Fori(0, KA - 1) as a:
            pair(Span(PAIR_UNITS, PAIR_UNITS, a), a + 1, a)

        at = Span(U_CONV)
        act.wait_ge(s_unit, U_CONV)
        for m in range(KA, KT):
            act.wait_ge(s_conv, m - KA + 1)
            operand_hi(m, hid[:, m, :], ROWS["attn"]).then_inc(s_xhi, 1)
        for i in range(KT):
            split(at, i + HILO)
            if i == 0:
                act.wait_ge(s_nsum, 1)
                on(rstd[:, 0:HALF], aux[:, BANK_D, 0:HALF], ACT.Sqrt, bias=EPS, scale=1.0 / D_CONV)
                on(rstd[:, HALF:T], aux[:, BANK_O, 0:HALF], ACT.Sqrt, bias=EPS, scale=1.0 / D_CONV).then_inc(s_nroot, 1)
            if i < PAIR_UNITS:
                attention(KA - 1, i)
            if i < KA - 1:
                operand_hi(i, hid[:, i, :], ROWS["attn"]).then_inc(s_xhi, 1)
            if i == 10:
                act.wait_ge(s_o, 2 * KA)
                act.wait_ge(s_out, 4 * KA)
                operand_hi(KA - 1, hid[:, KA - 1, :], ROWS["attn"]).then_inc(s_xhi, 1)
            if i == 13:
                act.wait_ge(s_nsum, 2)
                root_of(rstd_attn, D_ATTN).then_inc(s_nroot, 1)

        with act.Fori(0, 2) as i:
            at = Span(U_ATTN, 4, i)
            for b in range(4):
                split(at, b + HILO)
                m = i * 4 + (KA + b)
                act.wait_ge(s_h, i * 4 + (KT + b + 1))
                operand_hi(m, hid[:, m, :], ROWS["ffn"]).then_inc(s_xhi, 1)
        with act.Fori(0, 2) as i:
            at = Span(U_ATTN + 8, 4, i)
            for b in range(4):
                split(at, b + HILO)
        act.wait_ge(s_unit, U_FFN)
        act.wait_ge(s_h, 2 * KT)
        for m in range(KA):
            operand_hi(m, hid[:, m, :], ROWS["ffn"]).then_inc(s_xhi, 1)

        def f_tile(at, c, f, fresh=False):
            n = f + c * CHUNK
            split(at, HILO)
            split(at, HILO + 1)
            if fresh:
                act.wait_ge(s_nsum, 3)
                root_of(rstd, D_MODEL).then_inc(s_nroot, 1)
            act.wait_ge(s_read, f * 2 + (T_FFN + c * CHUNK_TILES + 1))
            on(act_t[:, :], res[:, 0, :], ACT.Sigmoid).then_inc(s_sig, 1)
            split(at, HILO + 2)
            split(at, HILO + 3)
            act.wait_ge(s_f, n * 2 + 2)
            on(fhi[:, f, :], res[:, 0, :], ACT.Copy).then_inc(s_fhi, 1)

        for c in range(CHUNKS):
            first = U_FFN + c * CHUNK_UNITS
            if c == 0:
                f_tile(Span(first), 0, 0, fresh=True)
                with act.Fori(0, CHUNK - 1) as f:
                    f_tile(Span(first + 4, 4, f), c, f + 1)
            else:
                with act.Fori(0, CHUNK) as f:
                    f_tile(Span(first, 4, f), c, f)
            with act.Fori(0, KT // 2) as i:
                at = Span(first + 4 * CHUNK, 4, i)
                for b in range(2):
                    split(at, HILO + 2 * b)
                    split(at, HILO + 2 * b + 1)
                    if c == CHUNKS - 1:
                        m = i * 2 + b
                        act.wait_ge(s_read, i * 2 + (T_PLE - KT + b + 1))
                        operand_hi(m, hid[:, m, :], ROWS["ple"]).then_inc(s_xhi, 1)

        def copy_y(n, slot):
            act.wait_ge(s_ytr, n)
            on(y_nat[:, slot, :, :], aux[:, BANK_S, :].rearrange("p (b f) -> p b f", b=QB), ACT.Copy).then_inc(s_ycp, 1)
            on(ys_nat[:, slot, :], aux[0:DEC, BANK_D, 0:P], ACT.Copy).then_inc(s_ycp, 1)

        def embed(i, first_turn, last_turn):
            at = Span(U_PLE, 12, i)
            for b in range(4):
                m = i * 4 + b
                fresh = first_turn and b == 0
                for u in range(3 * b, 3 * b + 3):
                    if not last_turn or u + HILO < 12:
                        split(at, u + HILO)
                    if u == 3 * b:
                        if fresh:
                            act.wait_ge(s_ptr, 1)
                            act.wait_ge(s_unit, U_PLE)
                            for t in range(KP):
                                on(phi[:, t, 0:SEQ], aux[:, BANK_T + t, :], ACT.Copy)
                                on(phi[:, t, SEQ:T], aux[:, BANK_D, t * DEC:(t + 1) * DEC], ACT.Copy).then_inc(s_phi, 1)
                        else:
                            if not (first_turn and b < 3):
                                act.wait_ge(d_y[(b - 1) % 2], i * 64 + ((b - 3) // 2 + 1) * 32)
                            copy_y(m, (b - 1) % 2)
                    if u == 3 * b + 1:
                        if fresh:
                            act.wait_ge(s_nsum, 4)
                            root_of(rstd, D_MODEL).then_inc(s_nroot, 1)
                        act.wait_ge(s_read, m * 2 + (T_PLE + 1))
                        on(act_t[:, :], res[:, 0, :], ACT.Sigmoid).then_inc(s_sig, 1)

        embed(0, True, False)
        with act.Fori(1, KT // 4 - 1) as i:
            embed(i, False, False)
        embed(KT // 4 - 1, False, True)
        act.wait_ge(d_y[1], (KT // 2 - 1) * 32)
        copy_y(KT, 1)

    @block.vector
    def _(dve):
        V = nc.vector

        def split(at, u):
            dve.wait_ge(s_whi, at.count(u))
            V.tensor_tensor(wlo[:, u % HILO, :], wraw[:, u % RAW, :], whi[:, u % HILO, :].bitcast(F32),
                            ALU.subtract).then_inc(s_wlo, 1)

        def scaled(out, slot, by):
            return V.tensor_tensor(halves(out), acc_of(slot), halves(by[:, :]), ALU.mult)

        def operand_lo(m, source, gain):
            return V.scalar_tensor_tensor(xlo[:, m, :], source, cols[:, bass.ds(m + gain, 1)],
                                          xhi[:, m, :].bitcast(F32), ALU.mult, ALU.subtract)

        def attention(a, g):
            if g == 0 or g == 1:
                e = g
                if g == 1:
                    dve.wait_ge(s_qb, 2 * a + 1)
                    dve.wait_ge(l_kc, 16 * a + 16)
                    keys_times_q(0).then_inc(s_mul, 1)
                dve.wait_ge(s_cols, 3 * a + 3)
                V.tensor_tensor(qdiag[:, :, :], ident[:, :].unsqueeze(1).broadcast_to([P, 4, P]),
                                qkv_s[:, 0, 4 * e:4 * e + 4].unsqueeze(2).broadcast_to([P, 4, P]),
                                ALU.mult).then_inc(s_qd, 1)
            if 1 <= g <= 8:
                c = g - 1
                w = (c % QB + 1) * P
                dve.wait_ge(s_pthi, 8 * a + (c + 1))
                V.tensor_tensor(ptlo[:, c % 2, 0:w], aux[:, BANK_T, 0:w], pthi[:, c % 2, 0:w].bitcast(F32),
                                ALU.subtract).then_inc(s_pt2, 1)
            if g == 5 or g == 9:
                e = (g - 5) // 4
                dve.wait_ge(s_pv, 8 * a + 4 * (e + 1))
                V.tensor_copy(hid[e * HD:(e + 1) * HD, a, 0:SEQ], aux[e * HD:(e + 1) * HD, BANK_O, :]).then_inc(s_o, 1)
            if g <= 7:
                e, w = g // QB, (g % QB + 1) * P
                buf = prob[:, g % 2, 0:w]
                if g == 0:
                    dve.wait_ge(l_skew, 16 * a + 16)
                if g >= 2:
                    dve.wait_ge(s_pt, 8 * a + (g - 1))
                dve.wait_ge(s_score, 8 * a + (g + 1))
                V.scalar_tensor_tensor(buf, aux[:, BANK_S, 0:w], HD ** -0.5, skew[:, e, SEQ - w:SEQ],
                                       ALU.mult, ALU.add).then_inc(s_biased, 1)
                dve.wait_ge(s_biased, 8 * a + (g + 1))
                V.tensor_reduce(stats[:, 0:1], buf, X, ALU.max).then_inc(s_max, 1)
                dve.wait_ge(s_max, 8 * a + (g + 1))
                V.tensor_scalar(stats[:, 1:2], stats[:, 0:1], -1.0, None, ALU.mult).then_inc(s_nmax, 1)
            if g == 2:
                dve.wait_ge(s_qb, 2 * a + 2)
                keys_times_q(1).then_inc(s_mul, 1)
                dve.wait_ge(s_mul, 2 * a + 2)
                for t in range(KCACHE):
                    V.tensor_reduce(key_sc[:, t, :].rearrange("p (b e) -> p b e", b=DEC),
                                    kv.rearrange("p (b t) (e d) -> p b t e d", t=KCACHE, e=2)[:, :, t, :, :],
                                    X, ALU.add).then_inc(s_key, 1)
                V.tensor_tensor(kq_s[:, :], qkv_s[:, 0, :], qkv_s[:, 1, :], ALU.mult).then_inc(s_key, 1)
                dve.wait_ge(s_key, 4 * a + 3)
                V.tensor_tensor(kq_pair[:, :, :], kq_s[:, :].unsqueeze(2).broadcast_to([P, DEC, 2]),
                                half_mask[:, :].unsqueeze(1).broadcast_to([P, DEC, 2]), ALU.mult).then_inc(s_key, 1)
            if g == 3:
                dve.wait_ge(l_row, 16 * a + 16)
                dve.wait_ge(s_str, 2 * a + 1)
                V.scalar_tensor_tensor(row[:, :], aux[0:2 * DEC, BANK_D, 0:ROW_W], HD ** -0.5, row_bias[:, :],
                                       ALU.mult, ALU.add).then_inc(s_row, 1)
                dve.wait_ge(s_row, 6 * a + 1)
                V.tensor_reduce(row_stats[:, 0:1], row[:, :], X, ALU.max).then_inc(s_row, 1)
                dve.wait_ge(s_row, 6 * a + 2)
                V.tensor_scalar(row_stats[:, 1:2], row_stats[:, 0:1], -1.0, None, ALU.mult).then_inc(s_row, 1)
            if g == 4:
                dve.wait_ge(s_sexp, a + 1)
                V.reciprocal(row_stats[:, 3:4], row_stats[:, 2:3]).then_inc(s_row, 1)
                dve.wait_ge(s_row, 6 * a + 4)
                V.tensor_scalar(row[:, :], row[:, :], row_stats[:, 3:4], None, ALU.mult).then_inc(s_row, 1)
                dve.wait_ge(s_row, 6 * a + 5)
                V.tensor_scalar(new_diag[:, :], ident[0:2 * DEC, 0:2 * DEC], row[:, PAST:PAST + 1], None,
                                ALU.mult).then_inc(s_row, 1)
            if g == 5:
                dve.wait_ge(s_str, 2 * a + 2)
                V.tensor_copy(p_cols.rearrange("p t c -> p (t c)"), aux[:, BANK_D, 0:3 * 2 * DEC]).then_inc(s_pc, 1)
            if g == 6:
                dve.wait_ge(s_pc, a + 1)
                V.tensor_tensor(out_s[:, :, :], qkv_s[:, 2, :].unsqueeze(2).broadcast_to([P, DEC, 2]),
                                p_cols[:, KCACHE, :].rearrange("p (b e) -> p b e", b=DEC), ALU.mult).then_inc(s_out, 1)
                dve.wait_ge(s_out, 4 * a + 1)
                dve.wait_ge(s_spv, a + 1)
                V.tensor_tensor(out_s[:, :, :], out_s[:, :, :],
                                aux[:, BANK_D, 0:2 * DEC].rearrange("p (b e) -> p b e", b=DEC), ALU.add).then_inc(s_out, 1)
                dve.wait_ge(s_out, 4 * a + 2)
                for e in range(2):
                    V.tensor_copy(hid[e * HD:(e + 1) * HD, a, SEQ:T], out_s[e * HD:(e + 1) * HD, :, e]).then_inc(s_out, 1)
            if g <= 7:
                buf = prob[:, g % 2, 0:(g % QB + 1) * P]
                dve.wait_ge(s_exp, 8 * a + (g + 1))
                V.reciprocal(stats[:, 3:4], stats[:, 2:3]).then_inc(s_rden, 1)
                dve.wait_ge(s_rden, 8 * a + (g + 1))
                V.tensor_scalar(buf, buf, stats[:, 3:4], None, ALU.mult).then_inc(s_prob, 1)

        def keys_times_q(e):
            part = kv.rearrange("p (b t) f -> p b t f", t=KCACHE)[:, 4 * e:4 * e + 4, :, :]
            return V.tensor_tensor(part, part, aux[:, BANK_D, :].rearrange("p (b f) -> p b f", b=4)
                                   .unsqueeze(2).broadcast_to([P, 4, KCACHE, P]), ALU.mult)

        def heads(j, a, g):
            if g == 1:
                if a is None:
                    dve.wait_ge(s_rsb, 1)
                    V.tensor_copy(rstd[:, 0:SEQ], aux[:, BANK_S, :]).then_inc(s_rstd, 1)
                    V.tensor_copy(rstd[:, SEQ:T], aux[:, BANK_D, 0:DEC]).then_inc(s_rstd, 1)
                    dve.wait_ge(s_rstd, 2)
                    dve.wait_ge(d_bias, 16)
                    V.memset(u_t[:, 0:2], 0.0).then_inc(s_zero, 1)
                    dve.wait_ge(s_zero, 1)
                dve.wait_ge(s_unit, 12 * j + 2)
                scaled(v_t[:, :], 0, rstd).then_inc(s_read, 1)
            if g == 3:
                dve.wait_ge(s_unit, 12 * j + 4)
                if a is not None:
                    dve.wait_ge(s_nat, 2 * j)
                scaled(k_t[:, :], 1, rstd).then_inc(s_read, 1)
            if g == 5:
                dve.wait_ge(s_unit, 12 * j + 6)
                if a is not None:
                    dve.wait_ge(s_qkhi, 2 * j)
                scaled(q_t[:, :], 0, rstd).then_inc(s_read, 1)
            if g == 7:
                dve.wait_ge(s_unit, 12 * j + 8)
                if a is not None:
                    dve.wait_ge(s_conv, j)
                scaled(conv[:, :], 1, rstd).then_inc(s_read, 1)
            if g == 9:
                dve.wait_ge(s_unit, 12 * j + 10)
                scaled(gate_t[:, :], 0, rstd).then_inc(s_read, 1)
                dve.wait_ge(s_read, 6 * j + 5)
                V.tensor_tensor(u_t[:, 2:2 + T], conv[:, :], gate_t[:, :], ALU.mult).then_inc(s_u, 1)
                norm_head(k_t, ROWS["k"], 2 * j)
                V.tensor_copy(qkv_s[:, 1, :], k_t[:, SEQ:T]).then_inc(s_cols, 1)
                dve.wait_ge(s_qkhi, 2 * j + 1)
                V.tensor_tensor(klo[:, :], k_t[:, 0:SEQ], khi[:, :].bitcast(F32), ALU.subtract).then_inc(s_qk2, 1)
            if g == 10:
                norm_head(q_t, ROWS["q"], 2 * j + 1)
                V.tensor_copy(qkv_s[:, 0, :], q_t[:, SEQ:T]).then_inc(s_cols, 1)
                V.tensor_copy(qkv_s[:, 2, :], v_t[:, SEQ:T]).then_inc(s_cols, 1)
                dve.wait_ge(s_vhi, j + 1)
                V.tensor_tensor(vlo[:, :, :], v_nat[:, :, :], vhi[:, :, :].bitcast(F32), ALU.subtract).then_inc(s_v2, 1)
                dve.wait_ge(s_qkhi, 2 * j + 2)
                V.tensor_tensor(qlo[:, :], q_t[:, 0:SEQ], qhi[:, :].bitcast(F32), ALU.subtract).then_inc(s_qk2, 1)

                def tap(t):
                    return cols[:, bass.ds(j + (ROWS["taps"] + t * KC), 1)]

                old = state_t[:, j, :].rearrange("p (b t) -> p b t", t=2)
                dve.wait_ge(s_u, j + 1)
                V.tensor_scalar(conv[:, :], u_t[:, 2:2 + T], tap(2), None, ALU.mult).then_inc(s_tap, 1)
                for n, t in enumerate((1, 0)):
                    dve.wait_ge(s_tap, 5 * j + (2 * n + 1))
                    V.scalar_tensor_tensor(conv[:, 0:SEQ], u_t[:, t:t + SEQ], tap(t), conv[:, 0:SEQ],
                                           ALU.mult, ALU.add).then_inc(s_tap, 1)
                    V.scalar_tensor_tensor(conv[:, SEQ:T], old[:, :, t], tap(t), conv[:, SEQ:T],
                                           ALU.mult, ALU.add).then_inc(s_tap, 1)
            if g == 11:
                dve.wait_ge(s_unit, 12 * j + 12)
                scaled(gate_t[:, :], 1, rstd).then_inc(s_read, 1)
                dve.wait_ge(s_read, 6 * j + 6)
                dve.wait_ge(s_tap, 5 * j + 5)
                if a is None:
                    dve.wait_ge(d_spill, 16)
                V.tensor_tensor(hid[:, j + KA, :], conv[:, :], gate_t[:, :], ALU.mult).then_inc(s_conv, 1)

        def norm_head(tile, gain, n):
            dve.wait_ge(s_root, n + 1)
            V.reciprocal(qk_rstd[:, :], qk_rstd[:, :]).then_inc(s_inv, 1)
            dve.wait_ge(s_inv, n + 1)
            V.scalar_tensor_tensor(tile[:, :], tile[:, :], cols[:, gain:gain + 1], qk_rstd[:, :],
                                   ALU.mult, ALU.mult).then_inc(s_qk, 1)
            dve.wait_ge(s_qk, n + 1)

        def pair(at, j, a):
            for g in range(PAIR_UNITS):
                split(at, g + HILO)
                if a is not None:
                    attention(a, g)
                heads(j, a, g)

        V.memset(ones[:, :], 1.0).then_inc(s_const, 1)
        V.memset(rel[BUCKETS:BUCKETS + 1, :], 1.0).then_inc(s_const, 1)
        V.memset(acc_conv[:, :], 0.0).then_inc(s_const, 1)
        V.memset(acc_attn[:, :], 0.0).then_inc(s_const, 1)
        for e in range(2):
            for d in range(2):
                V.memset(headsum[e * HD:(e + 1) * HD, d * HD:(d + 1) * HD], float(e == d)).then_inc(s_const, 1)
                V.memset(half_mask[e * HD:(e + 1) * HD, d:d + 1], float(e == d)).then_inc(s_const, 1)
        for t in range(KT):
            if t == 0:
                dve.wait_ge(s_cp0, 2)
            dve.wait_ge(s_xt, t + 1)
            gain = cols[:, ROWS["mix"] + t:ROWS["mix"] + t + 1]
            V.tensor_scalar(xhi[:, t, :], hid[:, t, :], gain, None, ALU.mult).then_inc(s_xhi, 1)
            dve.wait_ge(s_xhi, t + 1)
            operand_lo(t, hid[:, t, :], ROWS["mix"]).then_inc(s_x, 1)
            if t == 3:
                split(FIRST, 0)
            if t == 9:
                split(FIRST, 1)
        dve.wait_ge(s_const, CONSTANTS)
        dve.wait_ge(s_xrs, 2)
        V.reciprocal(x_rs[:, 0:QB], x_rs[:, 0:QB]).then_inc(s_xrstd, 1)
        V.reciprocal(x_rs[0:DEC, QB:QB + 1], x_rs[0:DEC, QB:QB + 1]).then_inc(s_xrstd, 1)
        dve.wait_ge(s_xrstd, 2)
        V.tensor_tensor(xdiag[:, :, :], ident[:, :].unsqueeze(1).broadcast_to([P, QB, P]),
                        x_rs[:, 0:QB].unsqueeze(2).broadcast_to([P, QB, P]), ALU.mult).then_inc(s_xdiag, 1)
        V.tensor_scalar(xsdiag[:, :], ident[0:DEC, 0:DEC], x_rs[0:DEC, QB:QB + 1], None, ALU.mult).then_inc(s_xdiag, 1)
        split(FIRST, 2)
        split(FIRST, 3)

        pair(FIRST, 0, None)
        with dve.Fori(0, KA - 1) as a:
            pair(Span(PAIR_UNITS, PAIR_UNITS, a), a + 1, a)

        at = Span(U_CONV)
        for m in range(KA, KT):
            dve.wait_ge(s_xhi, KT + m - KA + 1)
            operand_lo(m, hid[:, m, :], ROWS["attn"]).then_inc(s_x, 1)
        for i in range(KT):
            m = (KA + i) % KT
            split(at, i + HILO)
            if i < PAIR_UNITS:
                attention(KA - 1, i)
            if i < KA - 1 or i == 10:
                t = min(i, KA - 1)
                dve.wait_ge(s_xhi, KT + KC + t + 1)
                operand_lo(t, hid[:, t, :], ROWS["attn"]).then_inc(s_x, 1)
            if i == 0:
                dve.wait_ge(s_nroot, 1)
                V.reciprocal(rstd[:, :], rstd[:, :]).then_inc(s_ninv, 1)
                dve.wait_ge(s_ninv, 1)
            dve.wait_ge(s_unit, U_CONV + i + 1)
            if i > 0:
                dve.wait_ge(s_h, i)
            scaled(act_t[:, :], i % 2, rstd).then_inc(s_read, 1)
            dve.wait_ge(s_read, T_CONV + i + 1)
            dve.wait_ge(l_res[i % 2], 16 * (i // 2 + 1))
            V.tensor_tensor(hid[:, m, :], act_t[:, :], res[:, i % 2, :], ALU.add).then_inc(s_h, 1)
            if i == 14:
                dve.wait_ge(s_nroot, 2)
                V.reciprocal(rstd_attn[:, :], rstd_attn[:, :]).then_inc(s_ninv, 1)

        dve.wait_ge(s_ninv, 2)
        for part in range(2):
            with dve.Fori(0, 2) as i:
                at = Span(U_ATTN + 8 * part, 4, i)
                for b in range(4):
                    n = i * 4 + (8 * part + b)
                    m = i * 4 + (KA * (1 - part) + b)
                    split(at, b + HILO)
                    dve.wait_ge(s_unit, n + (U_ATTN + 1))
                    dve.wait_ge(s_h, n + KT)
                    scaled(act_t[:, :], b % 2, rstd_attn).then_inc(s_read, 1)
                    dve.wait_ge(s_read, n + (T_ATTN + 1))
                    V.tensor_tensor(hid[:, m, :], act_t[:, :], hid[:, m, :], ALU.add).then_inc(s_h, 1)
                    if part == 0:
                        dve.wait_ge(s_xhi, n + (2 * KT + 1))
                        operand_lo(m, hid[:, m, :], ROWS["ffn"]).then_inc(s_x, 1)
        for m in range(KA):
            dve.wait_ge(s_xhi, 2 * KT + KA + m + 1)
            operand_lo(m, hid[:, m, :], ROWS["ffn"]).then_inc(s_x, 1)

        def f_tile(at, c, f, fresh=False):
            n = f + c * CHUNK
            split(at, HILO)
            split(at, HILO + 1)
            if fresh:
                dve.wait_ge(s_nroot, 3)
                V.reciprocal(rstd[:, :], rstd[:, :]).then_inc(s_ninv, 1)
                dve.wait_ge(s_ninv, 3)
            else:
                dve.wait_ge(s_f2, n)
            dve.wait_ge(s_unit, at.count(1))
            scaled(res[:, 0, :], 0, rstd).then_inc(s_read, 1)
            split(at, HILO + 2)
            split(at, HILO + 3)
            dve.wait_ge(s_unit, at.count(3))
            scaled(res[:, 1, :], 1, rstd).then_inc(s_read, 1)
            dve.wait_ge(s_sig, n + 1)
            V.tensor_tensor(res[:, 0, :], res[:, 0, :], act_t[:, :], ALU.mult).then_inc(s_f, 1)
            dve.wait_ge(s_f, n * 2 + 1)
            dve.wait_ge(s_read, f * 2 + (T_FFN + c * CHUNK_TILES + 2))
            V.tensor_tensor(res[:, 0, :], res[:, 0, :], res[:, 1, :], ALU.mult).then_inc(s_f, 1)
            dve.wait_ge(s_fhi, n + 1)
            V.tensor_tensor(flo[:, f, :], res[:, 0, :], fhi[:, f, :].bitcast(F32), ALU.subtract).then_inc(s_f2, 1)

        for c in range(CHUNKS):
            first = U_FFN + c * CHUNK_UNITS
            if c == 0:
                f_tile(Span(first), 0, 0, fresh=True)
                with dve.Fori(0, CHUNK - 1) as f:
                    f_tile(Span(first + 4, 4, f), c, f + 1)
            else:
                with dve.Fori(0, CHUNK) as f:
                    f_tile(Span(first, 4, f), c, f)
            with dve.Fori(0, KT // 2) as i:
                at = Span(first + 4 * CHUNK, 4, i)
                for b in range(2):
                    m = i * 2 + b
                    split(at, HILO + 2 * b)
                    split(at, HILO + 2 * b + 1)
                    dve.wait_ge(s_unit, at.count(2 * b + 1))
                    V.tensor_tensor(halves(hid[:, m, :]), acc_of(b), halves(hid[:, m, :]), ALU.add).then_inc(s_read, 1)
                    if c == CHUNKS - 1:
                        dve.wait_ge(s_xhi, m + (3 * KT + 1))
                        operand_lo(m, hid[:, m, :], ROWS["ple"]).then_inc(s_x, 1)

        def embed(i, first_turn, last_turn):
            at = Span(U_PLE, 12, i)
            for b in range(4):
                m = i * 4 + b
                fresh = first_turn and b == 0
                for u in range(3 * b, 3 * b + 3):
                    if not last_turn or u + HILO < 12:
                        split(at, u + HILO)
                    if fresh and u == 0:
                        dve.wait_ge(s_phi, KP)
                        for t in range(KP):
                            V.tensor_tensor(plo[:, t, 0:SEQ], aux[:, BANK_T + t, :], phi[:, t, 0:SEQ].bitcast(F32),
                                            ALU.subtract)
                            V.tensor_tensor(plo[:, t, SEQ:T], aux[:, BANK_D, t * DEC:(t + 1) * DEC],
                                            phi[:, t, SEQ:T].bitcast(F32), ALU.subtract).then_inc(s_p2, 1)
                    if u == 3 * b + 1:
                        if fresh:
                            dve.wait_ge(s_nroot, 4)
                            V.reciprocal(rstd[:, :], rstd[:, :]).then_inc(s_ninv, 1)
                            dve.wait_ge(s_ninv, 4)
                        dve.wait_ge(s_unit, at.count(u))
                        scaled(res[:, 0, :], 0, rstd).then_inc(s_read, 1)
                    if u == 3 * b + 2:
                        dve.wait_ge(s_sig, m + (CHUNKS * CHUNK + 1))
                        if not fresh:
                            dve.wait_ge(s_ytr, m)
                            dve.wait_ge(s_y, m)
                        dve.wait_ge(s_unit, at.count(u))
                        V.tensor_tensor(halves(res[:, 1, :]), acc_of(1), halves(act_t[:, :]), ALU.mult).then_inc(s_read, 1)
                        dve.wait_ge(s_read, m * 2 + (T_PLE + 2))
                        V.tensor_tensor(y_t[:, :], res[:, 1, :], hid[:, m, :], ALU.add).then_inc(s_y, 1)

        embed(0, True, False)
        with dve.Fori(1, KT // 4 - 1) as i:
            embed(i, False, False)
        embed(KT // 4 - 1, False, True)

    @block.gpsimd
    def _(pool):
        G = nc.gpsimd

        def apart():
            pool.sem_inc(s_passed, 1)

        def add_squares(total, tile, before):
            pool.wait_ge(s_sqs, before)
            G.tensor_tensor(gsq[:, :], tile, tile, ALU.mult).then_inc(s_sqs, 1)
            pool.wait_ge(s_sqs, before + 1)
            G.tensor_tensor(total[:, :], total[:, :], gsq[:, :], ALU.add).then_inc(s_sqs, 1)

        def load_keys(a):
            pool.dma_start(kv[:, :, :], cache_k[0].rearrange("b (t p) h d -> p (b t) (h d)", p=P)[
                :, :, bass.ts(a, P)]).then_inc(l_kc, 16)

        def load_bias(a):
            pool.dma_start(row_bias[:, :], row_dram[a].rearrange("b e i -> (b e) i")).then_inc(l_row, 16)

        def load_skew(a):
            pool.dma_start(skew[:, :, :], skew_dram[bass.ds(a * 2, 2)].rearrange("e p y -> p e y")).then_inc(l_skew, 16)

        def load_values(a):
            pool.wait_ge(s_key, 4 * a + 2)
            apart()
            pool.dma_start(kv[:, :, :], cache_v[0].rearrange("b (t p) h d -> p (b t) (h d)", p=P)[
                :, :, bass.ts(a, P)]).then_inc(l_vc, 16)

        def attention(a):
            load_values(a)
            pool.wait_ge(s_row, 6 * a + 1)
            apart()
            load_bias(a + 1)
            pool.wait_ge(s_spv, a + 1)
            apart()
            load_keys(a + 1)
            pool.wait_ge(s_biased, 8 * a + 8)
            apart()
            load_skew(a + 1)
            pool.wait_ge(s_o, 2 * a + 2)
            pool.wait_ge(s_out, 4 * a + 4)
            add_squares(acc_attn, hid[:, a, :], 4 * a + 2)

        def store_rows(j):
            at = bass.ts(j, P)
            pool.wait_ge(s_natsb, 5 * j + 1)
            apart()
            pool.dma_start(v_prompt[0, 0].rearrange("(b p) h d -> p b (h d)", p=P)[:, :, at], v_nat[:, :, :]
                           ).then_inc(d_v, 16)
            pool.wait_ge(s_natsb, 5 * j + 3)
            apart()
            pool.dma_start(k_prompt[0, 0].rearrange("(b p) h d -> p b (h d)", p=P)[:, :, at], k_nat[:, :, :]
                           ).then_inc(d_k, 16)
            pool.wait_ge(s_natsb, 5 * j + 5)
            apart()
            pool.dma_start(v_sample[0, :, 0].rearrange("b h d -> b (h d)")[:, at], small_nat[0:DEC, 0, :]
                           ).then_inc(d_small, 16)
            pool.dma_start(k_sample[0, :, 0].rearrange("b h d -> b (h d)")[:, at], small_nat[0:DEC, 1, :]
                           ).then_inc(d_small, 16)
            pool.dma_start(conv_prompt[0, 0][:, at], small_nat[0:2, 2, :]).then_inc(d_small, 16)
            pool.dma_start(conv_sample[0, :, 1, at], small_nat[2:DEC + 2, 2, :]).then_inc(d_small, 16)

        rows = gain_rows
        pool.dma_start(rows[0:KT, :], g_mix[0].rearrange("(t p) -> t p", p=P)).then_inc(l_rows, 16)
        pool.dma_start(rows[KT:2 * KT, :], g_ffn[0].rearrange("(t p) -> t p", p=P)).then_inc(l_rows, 16)
        pool.dma_start(rows[2 * KT:3 * KT, :], g_ple[0].rearrange("(t p) -> t p", p=P)).then_inc(l_rows, 16)
        pool.dma_start(rows[ROWS["attn"]:ROWS["conv"], :], g_attn_out[0].rearrange("(t p) -> t p", p=P)).then_inc(l_rows, 16)
        pool.dma_start(rows[ROWS["conv"]:ROWS["taps"], :], g_conv_out[0].rearrange("(t p) -> t p", p=P)).then_inc(l_rows, 16)
        pool.dma_start(rows[ROWS["taps"]:ROWS["q"], :], conv_w[0].rearrange("c (t p) -> (c t) p", p=P)).then_inc(l_rows, 16)
        for e in range(2):
            pool.dma_start(rows[ROWS["q"]:ROWS["q"] + 1, e * HD:(e + 1) * HD], q_norm).then_inc(l_rows, 16)
            pool.dma_start(rows[ROWS["k"]:ROWS["k"] + 1, e * HD:(e + 1) * HD], k_norm).then_inc(l_rows, 16)
        pool.dma_start(xs_nat[:, :], x_sample[:, 0, :]).then_inc(l_xs, 16)
        pool.dma_start(state_nat[:, :], state_conv[0].rearrange("b t c -> (b t) c")).then_inc(l_state, 16)
        pool.dma_start(rel[0:BUCKETS, :], rel_bias).then_inc(l_table, 16)
        pool.dma_start(table_sb[:, :], table).then_inc(l_table, 16)
        pool.dma_start(conv_sample[0, :, 0, :], state_conv[0, :, 1, :]).then_inc(d_state, 16)
        G.memset(ident[:, :], 0.0).then_inc(s_ident, 1)
        pool.wait_ge(s_ident, 1)
        G.affine_select(out=ident[:, :], in_=ident[:, :], compare_op=ALU.not_equal, fill=1.0, base=0,
                        pattern=[[-1, P]], channel_multiplier=1).then_inc(s_const, 1)
        pool.wait_ge(s_xt, KT)
        pool.wait_ge(s_cp0, 2)
        pool.dma_start(xt_dram, hid[:, :, :]).then_inc(d_spill, 16)
        pool.wait_ge(s_cp0, 4)
        pool.dma_start(bias_dram, bias_sb[:, :]).then_inc(d_bias, 16)
        pool.wait_ge(d_bias, 16)
        shifted = bias_dram[:, P - 1:P - 1 + SEQ]
        shifted = bass.AP(tensor=shifted.tensor, offset=shifted.offset, ap=[[BIAS_W, HEADS], [-1, P], [1, SEQ]])
        pool.dma_start(skew_dram, shifted).then_inc(d_skew, 16)
        for b in range(DEC):
            pool.dma_start(row_dram[:, b, :, :], bias_dram[:, PAST - 1:PAST - 1 + ROW_W].rearrange(
                "(j e) i -> j e i", e=2)).then_inc(d_rows, 16)
        pool.wait_ge(s_rsb, 1)
        load_keys(0)
        pool.wait_ge(d_rows, 16 * DEC)
        load_bias(0)
        pool.wait_ge(d_skew, 16)
        load_skew(0)
        pool.wait_ge(s_const, CONSTANTS)

        store_rows(0)
        pool.wait_ge(s_conv, 1)
        G.tensor_tensor(gsq[:, :], hid[:, KA, :], hid[:, KA, :], ALU.mult).then_inc(s_sqs, 1)
        pool.wait_ge(s_sqs, 1)
        G.tensor_tensor(acc_conv[:, :], acc_conv[:, :], gsq[:, :], ALU.add).then_inc(s_sqs, 1)
        with pool.Fori(0, KA - 1) as a:
            attention(a)
            store_rows(a + 1)
            pool.wait_ge(s_conv, a + 2)
            add_squares(acc_conv, hid[:, a + (KA + 1), :], 4 * a + 4)

        for i in range(KT):
            if i < 2:
                pool.wait_ge(s_conv, KC)
            else:
                pool.wait_ge(s_h, i - 1)
            pool.dma_start(res[:, i % 2, :], xt_dram[:, (KA + i) % KT, :]).then_inc(l_res[i % 2], 16)
            if i == 3:
                load_values(KA - 1)
            if i == 11:
                pool.wait_ge(s_o, 2 * KA)
                pool.wait_ge(s_out, 4 * KA)
                add_squares(acc_attn, hid[:, KA - 1, :], SQ_CONV)

        pool.wait_ge(s_nsum, 2)
        G.memset(acc_attn[:, :], 0.0).then_inc(s_zero, 1)
        pool.wait_ge(s_zero, 2)
        pool.wait_ge(d_v, 16 * KA)
        pool.wait_ge(d_k, 16 * KA)
        pool.wait_ge(d_small, 64 * KA)
        pool.dma_start(p_nat[:, :, :], p_prompt[0, 0].rearrange("(b p) f -> p b f", p=P)).then_inc(l_p, 16)
        pool.dma_start(ps_nat[:, :], p_sample[0, :, 0, :]).then_inc(l_p, 16)
        for part in range(2):
            with pool.Fori(0, KA) as i:
                pool.wait_ge(s_h, i + (KT + KA * part + 1))
                add_squares(acc_attn, hid[:, i + KA * (1 - part), :], i * 2 + (SQ_ATTN + 2 * KA * part))

        pool.wait_ge(s_nsum, 3)
        G.memset(acc_attn[:, :], 0.0).then_inc(s_zero, 1)
        pool.wait_ge(s_zero, 3)
        with pool.Fori(0, KT) as m:
            pool.wait_ge(s_read, m + (T_PLE - KT + 1))
            add_squares(acc_attn, hid[:, m, :], m * 2 + SQ_FFN)

        with pool.Fori(0, KT // 2) as i:
            for b in range(2):
                m = i * 2 + b
                pool.wait_ge(s_ycp, i * 4 + (2 * b + 2))
                apart()
                pool.dma_start(y_prompt[0].rearrange("(b p) f -> p b f", p=P)[:, :, bass.ts(m, P)],
                               y_nat[:, b, :, :]).then_inc(d_y[b], 16)
                pool.dma_start(y_sample[:, 0, bass.ts(m, P)], ys_nat[:, b, :]).then_inc(d_y[b], 16)
        for b in range(2):
            pool.wait_ge(d_y[b], KT // 2 * 32)
        pool.wait_ge(d_state, 16)
        pool.wait_ge(d_spill, 16)

    ctx.close()


def kernel(**inputs):
    import concourse.bacc as bacc
    from concourse.bass_utils import run_bass_kernel_spmd as run

    nc = bacc.Bacc("TRN2", target_bir_lowering=False, num_devices=1)
    names = ("x_prompt", "x_sample", "p_prompt", "p_sample", "cache_k", "cache_v", "state_conv", "rel_bias",
             "g_mix", "w_in", "q_norm", "k_norm", "conv_w", "g_attn_out", "g_conv_out", "w_out", "g_ffn",
             "w_gate", "w_up", "w_down", "g_ple", "w_ple_gate", "w_ple_proj")
    arrays = {f"in_{n}": np.ascontiguousarray(inputs[n]) for n in names}
    arrays["in_table"] = bucket_table()
    args = [nc.dram_tensor(n, a.shape, mybir.dt.from_np(a.dtype), kind="ExternalInput").ap()
            for n, a in arrays.items()]
    outs = dict(y_prompt=(1, SEQ, D_MODEL), y_sample=(DEC, 1, D_MODEL), k_prompt=(1, 1, SEQ, HEADS, HD),
                v_prompt=(1, 1, SEQ, HEADS, HD), conv_prompt=(1, 1, 2, D_CONV), k_sample=(1, DEC, 1, HEADS, HD),
                v_sample=(1, DEC, 1, HEADS, HD), conv_sample=(1, DEC, 2, D_CONV))
    args += [nc.dram_tensor(f"out_{n}", s, F32, kind="ExternalOutput").ap() for n, s in outs.items()]
    build(nc, *args)
    got = run(nc, [arrays], core_ids=[0]).results[0]
    return tuple(got[f"out_{n}"] for n in outs)
```

```python
from contextlib import ExitStack

import numpy as np

import concourse.bass as bass
from concourse import mybir

F32 = mybir.dt.float32
F32R = mybir.dt.float32r
ALU = mybir.AluOpType
ACT = mybir.ActivationFunctionType
X = mybir.AxisListType.X

P = 128
D_MODEL, SEQ, DEC, PAST = 2048, 512, 8, 256
HEADS, HD = 16, 64
D_ATTN = HEADS * HD
D_CONV = D_MODEL - D_ATTN
D_FF, D_PLE = 5632, 256
BUCKETS, MAX_EXACT, MAX_DIST = 32, 16, 2048
DIL_STEPS, DILATIONS = 128, (1, 4, 16)
EPS = 1e-6
MASKED = -1e30

T = SEQ + DEC
HALF = T // 2
KT = D_MODEL // P
KA = D_ATTN // P
KC = D_CONV // P
QB = SEQ // P
KU = 8
UNIT = KU * P
RAW, HILO = 2, 4
CHUNK = 11
CHUNKS = D_FF // P // CHUNK
DOWN = (6, 5)
KCACHE = PAST // P
KP = D_PLE // P
BIAS_W = 640
ROW_W = PAST + 1
V_, K_, Q_, H_, C_, B_ = 2 * D_ATTN, D_ATTN, 0, 3 * D_ATTN, 3 * D_ATTN + 2 * D_CONV, 3 * D_ATTN + D_CONV
KINDS = (V_, K_, Q_, H_, C_, B_)
PAIR_UNITS = 2 * len(KINDS)
U_CONV = KA * PAIR_UNITS
U_ATTN = U_CONV + KT
U_FFN = U_ATTN + KT
CHUNK_UNITS = 4 * CHUNK + 2 * KT
U_PLE = U_FFN + CHUNKS * CHUNK_UNITS
PT = 4
U_GATE = U_PLE + KT // PT
T_CONV = KA * len(KINDS)
T_ATTN = T_CONV + KT
T_FFN = T_ATTN + KT
CHUNK_TILES = 2 * CHUNK + KT
T_PLE = T_FFN + CHUNKS * CHUNK_TILES
T_GATE = T_PLE + KT
ROWS = dict(mix=0, ffn=KT, ple=2 * KT, attn=3 * KT, conv=3 * KT + KA, taps=3 * KT + KA + KC)
ROWS["q"] = ROWS["taps"] + 3 * KC
ROWS["k"] = ROWS["q"] + 1
N_ROWS = ROWS["k"] + 1
SQ_X = KT
SQ_CONV = SQ_X + 2 * (KC + KA - 1)
SQ_ATTN = SQ_X + 2 * (KC + KA)
SQ_FFN = SQ_ATTN + 2 * KT
SQ_PLE = SQ_FFN + 2 * KT
N_X, N_CONV, N_ATTN, N_FFN, N_PLE = range(1, 6)
CONSTANTS = 13
PIECES = 8
XP = KT // PIECES
SMALL = 384
START_SPLITS = (2, 5, 9, 12)


def bucket_table():
    dist = SEQ - 1 - np.arange(BIAS_W)
    n = np.maximum(dist, 1)
    large = MAX_EXACT + (np.log(n.astype(np.float32) / MAX_EXACT)
                         / np.float32(np.log(MAX_DIST / MAX_EXACT)) * (BUCKETS - MAX_EXACT)).astype(np.int32)
    bucket = np.where(dist < MAX_EXACT, dist, np.minimum(large, BUCKETS - 1))
    count = sum(((dist >= 0) & (dist % d == 0) & (dist <= d * DIL_STEPS)).astype(int) for d in DILATIONS)
    table = np.zeros((BUCKETS + 1, BIAS_W), np.float32)
    for x in range(BIAS_W):
        if count[x]:
            table[bucket[x], x] = 1.0
            table[BUCKETS, x] = np.log(float(count[x]))
        else:
            table[BUCKETS, x] = MASKED
    return table


class Span:

    def __init__(self, first, per=0, turn=0):
        assert first % HILO == 0 and per % HILO == 0
        self.first, self.per, self.turn = first, per, turn

    def count(self, u):
        return self.turn * self.per + (self.first + u + 1)

    def landed(self, u):
        return self.turn * (16 * self.per // RAW) + 16 * ((self.first + u) // RAW + 1)


def build(nc, x_prompt, x_sample, p_prompt, p_sample, cache_k, cache_v, state_conv, rel_bias, g_mix,
          w_in, q_norm, k_norm, conv_w, g_attn_out, g_conv_out, w_out, g_ffn, w_gate, w_up, w_down,
          g_ple, w_ple_gate, w_ple_proj, table,
          y_prompt, y_sample, k_prompt, v_prompt, conv_prompt, k_sample, v_sample, conv_sample):
    w_in, w_out, w_gate, w_up, w_down = w_in[0], w_out[0], w_gate[0], w_up[0], w_down[0]
    w_ple_gate, w_ple_proj = w_ple_gate[0], w_ple_proj[0]

    xt_dram = nc.dram_tensor("xt_dram", (P, KT, T), F32, kind="Internal").ap()
    bias_dram = nc.dram_tensor("bias_dram", (HEADS, BIAS_W), F32, kind="Internal").ap()
    skew_dram = nc.dram_tensor("skew_dram", (HEADS, P, SEQ), F32, kind="Internal").ap()
    row_dram = nc.dram_tensor("row_dram", (KA, DEC, 2, ROW_W), F32, kind="Internal").ap()

    ctx = ExitStack()

    def sem(name):
        return ctx.enter_context(nc.semaphore(name))

    def sb(name, shape, dt=F32, scope=None):
        return (scope or ctx).enter_context(nc.sbuf_tensor(name, shape, dt))

    wraw = sb("wraw", [P, RAW, UNIT])
    whi = sb("whi", [P, HILO, UNIT], F32R)
    wlo = sb("wlo", [P, HILO, UNIT], F32R)
    xhi = sb("xhi", [P, KT, T], F32R)
    xlo = sb("xlo", [P, KT, T], F32R)
    hid = sb("hid", [P, KT, T])
    cols = sb("cols", [P, N_ROWS])
    ident = sb("ident", [P, P])
    ones = sb("ones", [P, P])
    rstd = sb("rstd", [P, T])
    gsq = sb("gsq", [P, T])
    tmp = sb("tmp", [P, 4, T])
    headsum = sb("headsum", [P, P])
    half_mask = sb("half_mask", [P, 2])
    state_t = sb("state_t", [P, KC, 2 * DEC])
    row = tmp[0:2 * DEC, 3, 0:ROW_W]
    conv, gate_t, sq, qk_rstd = (tmp[:, n, :] for n in range(4))
    res, act_t, acc_h = tmp[:, 0:2, :], tmp[:, 2, :], tmp[:, 3, :]

    mixers = ExitStack()
    sums = sb("sums", [P, 2, T], scope=mixers)
    acc_conv, acc_attn = sums[:, 0, :], sums[:, 1, :]
    rstd_attn = acc_conv

    mix = ExitStack()
    v_t = sb("v_t", [P, T], scope=mix)
    k_t = sb("k_t", [P, T], scope=mix)
    q_t = sb("q_t", [P, T], scope=mix)
    khi = sb("khi", [P, SEQ], F32R, mix)
    klo = sb("klo", [P, SEQ], F32R, mix)
    qhi = sb("qhi", [P, SEQ], F32R, mix)
    qlo = sb("qlo", [P, SEQ], F32R, mix)
    v_nat = sb("v_nat", [P, QB, P], scope=mix)
    k_nat = sb("k_nat", [P, QB, P], scope=mix)
    vhi = sb("vhi", [P, QB, P], F32R, mix)
    vlo = sb("vlo", [P, QB, P], F32R, mix)
    small_nat = sb("small_nat", [DEC + 2, 3, P], scope=mix)
    u_t = sb("u_t", [P, 2 + T], scope=mix)
    skew = sb("skew", [P, 2, SEQ], scope=mix)
    prob = sb("prob", [P, 2, SEQ], scope=mix)
    pthi = sb("pthi", [P, QB, 2, P], F32R, mix)
    ptlo = sb("ptlo", [P, QB, 2, P], F32R, mix)
    stats = sb("stats", [P, 3], scope=mix)
    kv = sb("kv", [P, DEC * KCACHE, P], scope=mix)
    qkv_s = sb("qkv_s", [P, 3, DEC], scope=mix)
    kq_s = sb("kq_s", [P, DEC], scope=mix)
    kq_pair = sb("kq_pair", [P, DEC, 2], scope=mix)
    key_sc = sb("key_sc", [P, KCACHE, 2 * DEC], scope=mix)
    row_bias = sb("row_bias", [2 * DEC, ROW_W], scope=mix)
    row_stats = sb("row_stats", [2 * DEC, 3], scope=mix)
    new_diag = sb("new_diag", [2 * DEC, 2 * DEC], scope=mix)
    p_cols = sb("p_cols", [P, 3, 2 * DEC], scope=mix)
    out_s = sb("out_s", [P, DEC, 2], scope=mix)
    mix.close()

    start = ExitStack()
    x_nat = sb("x_nat", [P, QB, D_MODEL], scope=start)
    xs_nat = sb("xs_nat", [DEC, D_MODEL], scope=start)
    mix_rows = sb("mix_rows", [KT, P], scope=start)
    gain_rows = sb("gain_rows", [N_ROWS - KT, P], scope=start)
    state_nat = sb("state_nat", [2 * DEC, D_CONV], scope=start)
    rel = sb("rel", [BUCKETS + 1, HEADS], scope=start)
    table_sb = sb("table_sb", [BUCKETS + 1, BIAS_W], scope=start)
    bias_sb = sb("bias_sb", [HEADS, BIAS_W], scope=start)
    start.close()
    mixers.close()

    ffn = ExitStack()
    phi = sb("phi", [P, KP, T], F32R, ffn)
    plo = sb("plo", [P, KP, T], F32R, ffn)
    hidden = ExitStack()
    fhi = sb("fhi", [P, CHUNK, T], F32R, hidden)
    flo = sb("flo", [P, CHUNK, T], F32R, hidden)
    hidden.close()
    before = ExitStack()
    p_nat = sb("p_nat", [P, QB, D_PLE], scope=before)
    ps_nat = sb("ps_nat", [DEC, D_PLE], scope=before)
    before.close()
    proj = sb("proj", [P, KT, T], scope=ffn)
    y_t = sb("y_t", [P, T], scope=ffn)
    y_nat = sb("y_nat", [P, 2, QB, P], scope=ffn)
    ys_nat = sb("ys_nat", [DEC, 2, P], scope=ffn)
    ffn.close()

    acc = ctx.enter_context(nc.psum_tensor("acc", [P, 2, 2, 512], F32))
    aux = ctx.enter_context(nc.psum_tensor("aux", [P, 4, 512], F32))
    BANK_S, BANK_D, BANK_T, BANK_O = range(4)

    def halves(tile):
        return tile.rearrange("p (h t) -> p h t", h=2)

    def acc_of(slot):
        return acc[:, slot, :, 0:HALF]

    aux_sum = aux[:, BANK_S:BANK_D + 1, 0:HALF]

    landed = [sem(f"unit_landed{i}") for i in range(RAW)]
    s_whi = sem("weights_hi_written")
    s_wlo = sem("weights_split")
    s_unit = sem("unit_multiplied")
    s_read = sem("product_read")
    s_x = sem("operand_tile_split")
    s_xhi = sem("operand_hi_written")
    l_rows, l_xs, l_table, l_state = sem("rows_landed"), sem("xs_landed"), sem("table_landed"), sem("state_landed")
    l_x = [sem(f"x_landed{g}") for g in range(PIECES)]
    l_mix = sem("mix_gain_landed")
    s_const, s_tr0, s_cp0, s_xt = sem("constants"), sem("start_transposed"), sem("start_copied"), sem("xt_copied")
    s_xsq = sem("x_squared")
    d_bias, d_skew, d_rows, d_spill = (sem("bias_stored"), sem("skew_stored"), sem("row_bias_stored"),
                                       sem("xt_stored"))
    d_state = sem("old_state_passed_on")
    s_sq, s_ssq, s_root, s_inv = sem("squared"), sem("heads_summed"), sem("root_ready"), sem("inverse_ready")
    s_qk, s_cols = sem("qk_normed"), sem("sample_cols")
    s_qkhi, s_qk2 = sem("qk_hi"), sem("qk_split")
    s_nat, s_natsb, s_vhi, s_v2 = sem("nat_transposed"), sem("nat_copied"), sem("v_hi"), sem("v_split")
    s_u, s_tap, s_conv = sem("u_ready"), sem("conv_tap"), sem("conv_ready")
    s_ident, s_sqs, s_zero, s_pad = (sem("identity_cleared"), sem("squares_step"), sem("squares_cleared"),
                                     sem("u_padded"))
    d_v, d_k, d_small = sem("v_stored"), sem("k_stored"), sem("small_stored")
    l_skew = sem("skew_landed")
    s_score, s_biased, s_nmax, s_exp = sem("scores"), sem("biased"), sem("row_max_negated"), sem("exponentials")
    s_rden, s_prob, s_pt, s_pthi, s_pt2, s_pv, s_o = (sem("row_sum_inverted"), sem("probabilities"),
                                                      sem("probs_transposed"), sem("probs_hi"), sem("probs_split"),
                                                      sem("values_weighted"), sem("attention_read"))
    l_kc, l_vc, l_row = sem("cached_k_landed"), sem("cached_v_landed"), sem("row_bias_landed")
    s_qb, s_mul, s_key, s_str, s_row, s_sexp, s_pc, s_spv, s_out = (
        sem("q_spread"), sem("keys_times_q"), sem("key_scores"), sem("samples_transposed"),
        sem("row_step"), sem("row_exponentials"), sem("prob_columns"), sem("cached_values_weighted"),
        sem("sample_step"))
    s_nsum, s_nroot, s_ninv = sem("norm_summed"), sem("norm_root"), sem("norm_rstd")
    l_res = [sem(f"residual_landed{i}") for i in range(2)]
    s_h = sem("h_tile_summed")
    s_sig, s_f, s_fhi, s_f2 = sem("sigmoid"), sem("hidden_step"), sem("hidden_hi"), sem("hidden_split")
    l_p, s_ptr, s_phi, s_p2 = sem("p_landed"), sem("p_transposed"), sem("p_hi"), sem("p_split")
    s_pm = sem("p_tile_multiplied")
    s_y, s_ytr, s_ycp = sem("y_step"), sem("y_transposed"), sem("y_copied")
    d_y = [sem(f"y_stored{i}") for i in range(2)]

    s_freed, s_passed = sem("sync_waits_passed"), sem("pool_waits_passed")

    FIRST = Span(0)
    block = ctx.enter_context(nc.Block())

    @block.sync
    def _(sp):
        def load(at, u, w, k0, nk, col, width=P):
            if not (at.first + u < RAW):
                sp.wait_ge(s_wlo, at.count(u) - RAW)
                sp.sem_inc(s_freed, 1)
            sp.dma_start(wraw[:, u % RAW, 0:nk * width].rearrange("p (k m) -> p k m", k=nk),
                         w[k0 * P:(k0 + nk) * P, bass.ds(col, width)].rearrange("(k p) m -> p k m", p=P)
                         ).then_inc(landed[u % RAW], 16)

        def pair(at, j):
            for n, kind in enumerate(KINDS):
                load(at, 2 * n, w_in, 0, KU, j * P + kind)
                load(at, 2 * n + 1, w_in, KU, KU, j * P + kind)

        sp.dma_start(x_nat[:, :, 0:XP * P], x_prompt[0, :, 0:XP * P].rearrange("(b p) f -> p b f", p=P)
                     ).then_inc(l_x[0], 16)
        pair(FIRST, 0)
        with sp.Fori(0, KA - 1) as a:
            pair(Span(PAIR_UNITS, PAIR_UNITS, a), a + 1)
        for part, m0 in enumerate((KT // 2, 0)):
            with sp.Fori(0, 2) as i:
                at = Span(U_CONV + part * KT // 2, 4, i)
                for b in range(4):
                    load(at, b, w_out, KA, KC, i * (4 * P) + (m0 + b) * P)
        with sp.Fori(0, KT // 4) as i:
            at = Span(U_ATTN, 4, i)
            for b in range(4):
                load(at, b, w_out, 0, KA, i * (4 * P) + b * P)

        def chunk_of(first, row0, col0):
            with sp.Fori(0, CHUNK) as f:
                at = Span(first, 4, f)
                for n, w in enumerate((w_gate, w_up)):
                    load(at, 2 * n, w, 0, KU, f * P + col0)
                    load(at, 2 * n + 1, w, KU, KU, f * P + col0)
            with sp.Fori(0, KT // 2) as i:
                at = Span(first + 4 * CHUNK, 4, i)
                for b in range(2):
                    load(at, b, w_down, row0, DOWN[0], i * (2 * P) + b * P)
                for b in range(2):
                    load(at, 2 + b, w_down, row0 + DOWN[0], DOWN[1], i * (2 * P) + b * P)

        for c in range(CHUNKS):
            chunk_of(U_FFN + c * CHUNK_UNITS, c * CHUNK, c * CHUNK * P)
        for i in range(KT // PT):
            load(Span(U_PLE), i, w_ple_proj, 0, KP, i * PT * P, PT * P)
        with sp.Fori(0, KT // 2) as i:
            at = Span(U_GATE, 4, i)
            for b in range(2):
                load(at, 2 * b, w_ple_gate, 0, KU, i * (2 * P) + b * P)
                load(at, 2 * b + 1, w_ple_gate, KU, KU, i * (2 * P) + b * P)

    @block.tensor
    def _(pe):
        mm = nc.tensor.matmul

        def unit(at, u, hi, lo, tiles, slot, first, last, ready=None, between=None):
            pe.wait_ge(s_wlo, at.count(u))
            for n, kt in enumerate(tiles):
                if between:
                    between(n)
                if ready:
                    pe.wait_ge(ready[0], ready[1] + n)
                w_h = whi[:, u % HILO, n * P:(n + 1) * P]
                w_l = wlo[:, u % HILO, n * P:(n + 1) * P]
                begin, end = first and n == 0, last and n == len(tiles) - 1
                for h in range(2):
                    mm(acc[:, slot, h, 0:HALF], w_h, hi[:, kt, h * HALF:(h + 1) * HALF], start=begin, stop=False)
                for h in range(2):
                    mm(acc[:, slot, h, 0:HALF], w_h, lo[:, kt, h * HALF:(h + 1) * HALF], start=False, stop=False)
                for h in range(2):
                    done = mm(acc[:, slot, h, 0:HALF], w_l, hi[:, kt, h * HALF:(h + 1) * HALF], start=False, stop=end)
            done.then_inc(s_unit, 1)

        def spread_sum(lhs, tile):
            for h in range(2):
                done = mm(aux[:, BANK_S + h, 0:HALF], lhs[:, :], tile[:, h * HALF:(h + 1) * HALF],
                          start=True, stop=True)
            return done

        def products(out, hi, lo, rhi, rlo, begin, end):
            mm(out, hi, rhi, start=begin, stop=False)
            mm(out, hi, rlo, start=False, stop=False)
            return mm(out, lo, rhi, start=False, stop=end)

        def attention(a, g):
            if g in (3, 5, 7, 9):
                pair_of = (g - 3) // 2
                q0 = pair_of % 2 * 2
                if pair_of == 0:
                    pe.wait_ge(s_v2, a + 1)
                if pair_of == 2:
                    pe.wait_ge(s_o, 2 * a + 1)
                pe.wait_ge(s_pt2, 8 * a + (2 * pair_of + 2))
                for kb in (0, q0 + 1, *range(1, q0 + 1)):
                    skip = kb > q0
                    done = products(aux[:, BANK_O, (q0 + skip) * P:(q0 + 2) * P], vhi[:, kb, :], vlo[:, kb, :],
                                    pthi[:, kb, skip:2, :], ptlo[:, kb, skip:2, :], kb == 0,
                                    kb == max(q0, 1))
                done.then_inc(s_pv, 1)
            if 1 <= g <= 8:
                c = g - 1
                if c == 0:
                    pe.wait_ge(s_natsb, 5 * a + 5)
                else:
                    pe.wait_ge(s_pt2, 8 * a + c)
                pe.wait_ge(s_prob, 8 * a + (c + 1))
                for kb in range(c % QB + 1):
                    done = nc.tensor.transpose(aux[:, BANK_T, kb * P:(kb + 1) * P],
                                               prob[:, c % 2, kb * P:(kb + 1) * P], ident[:, :])
                done.then_inc(s_pt, 1)
            if g <= 7:
                e, qb = g // QB, g % QB
                if g == 0:
                    pe.wait_ge(s_root, 2 * a + 2)
                    pe.wait_ge(s_qk2, 2 * a + 2)
                else:
                    pe.wait_ge(s_biased, 8 * a + g)
                rows = slice(e * HD, (e + 1) * HD)
                done = products(aux[:, BANK_S, 0:(qb + 1) * P],
                                qhi[rows, qb * P:(qb + 1) * P], qlo[rows, qb * P:(qb + 1) * P],
                                khi[rows, 0:(qb + 1) * P], klo[rows, 0:(qb + 1) * P], True, True)
                done.then_inc(s_score, 1)
            if g in (1, 2):
                if g == 1:
                    pe.wait_ge(s_cols, 3 * a + 3)
                if g == 2:
                    pe.wait_ge(s_mul, 2 * a + 1)
                for b in range(4):
                    n = 4 * (g - 1) + b
                    done = nc.tensor.transpose(aux[:, BANK_D, b * P:(b + 1) * P],
                                               qkv_s[:, 0, n:n + 1].broadcast_to([P, P]), ident[:, :])
                done.then_inc(s_qb, 1)
            if g == 5:
                pe.wait_ge(s_key, 4 * a + 4)
                for t in range(KCACHE):
                    nc.tensor.transpose(aux[0:2 * DEC, BANK_D, t * P:(t + 1) * P], key_sc[:, t, :], ident[:, :])
                mm(aux[0:2 * DEC, BANK_D, PAST:PAST + 1], kq_pair[:, :, :], ones[:, 0:1],
                   start=True, stop=True).then_inc(s_str, 1)
            if g == 7:
                pe.wait_ge(s_row, 5 * a + 5)
                mm(aux[:, BANK_D, KCACHE * 2 * DEC:(KCACHE + 1) * 2 * DEC], ones[0:2 * DEC, :], new_diag[:, :],
                   start=True, stop=True)
                for t in range(KCACHE):
                    done = nc.tensor.transpose(aux[:, BANK_D, t * 2 * DEC:(t + 1) * 2 * DEC],
                                               row[:, t * P:(t + 1) * P], ident[0:2 * DEC, 0:2 * DEC])
                done.then_inc(s_str, 1)
            if g == 8:
                pe.wait_ge(s_pc, a + 1)
                pe.wait_ge(l_vc, 16 * a + 16)
                for b in range(DEC):
                    for t in range(KCACHE):
                        done = mm(aux[:, BANK_D, 2 * b:2 * b + 2], kv[:, KCACHE * b + t, :],
                                  p_cols[:, t, 2 * b:2 * b + 2], start=t == 0, stop=t == KCACHE - 1)
                done.then_inc(s_spv, 1)

        def heads(j, a, g):
            if g == 9:
                if a is not None:
                    pe.wait_ge(s_biased, 8 * a + 8)
                    pe.wait_ge(s_out, 4 * a + 4)
                pe.wait_ge(s_sq, 2 * j + 1)
                spread_sum(headsum, sq).then_inc(s_ssq, 1)
            if g == 10:
                pe.wait_ge(s_root, 2 * j + 1)
                pe.wait_ge(s_sq, 2 * j + 2)
                spread_sum(headsum, sq).then_inc(s_ssq, 1)
                if a is not None:
                    pe.wait_ge(s_pt2, 8 * a + 8)
                    pe.wait_ge(s_o, 2 * a + 2)
                pe.wait_ge(s_read, 6 * j + 3)
                nc.tensor.transpose(aux[0:DEC, BANK_O, 0:P], v_t[:, SEQ:T], ident[:, :])
                for b in range(QB):
                    done = nc.tensor.transpose(aux[:, BANK_T, b * P:(b + 1) * P], v_t[:, b * P:(b + 1) * P],
                                               ident[:, :])
                done.then_inc(s_nat, 1)
            if g == 11:
                pe.wait_ge(s_natsb, 5 * j + 2)
                pe.wait_ge(s_qk, 2 * j + 1)
                pe.wait_ge(s_u, j + 1)
                nc.tensor.transpose(aux[0:DEC, BANK_O, P:2 * P], k_t[:, SEQ:T], ident[:, :])
                nc.tensor.transpose(aux[0:DEC + 2, BANK_O, 2 * P:3 * P], u_t[:, SEQ:SEQ + 2 + DEC], ident[:, :])
                for b in range(QB):
                    done = nc.tensor.transpose(aux[:, BANK_T, b * P:(b + 1) * P], k_t[:, b * P:(b + 1) * P],
                                               ident[:, :])
                done.then_inc(s_nat, 1)

        def pair(at, j, a):
            for g in range(PAIR_UNITS):
                n = g // 2
                if a is None and g == 1:
                    small_inputs()
                if g % 2 == 0 and (a is not None or n >= 2):
                    pe.wait_ge(s_read, 6 * j + (n - 1))
                if a is None and g == 2:
                    pe.wait_ge(s_cp0, 5)
                unit(at, g, xhi, xlo, range(g % 2 * KU, (g % 2 + 1) * KU), n % 2, g % 2 == 0, g % 2 == 1,
                     (s_x, g * KU + 1) if a is None and g < 2 else None,
                     transpose_later if a is None and g == 0 else None)
                if a is None and g == 4:
                    pe.wait_ge(s_xt, KT)
                    pe.wait_ge(s_sqs, SQ_X)
                    spread_sum(ones, acc_attn).then_inc(s_nsum, 1)
                if a is not None:
                    attention(a, g)
                heads(j, a, g)

        def transpose_x(t):
            if t % XP == 0:
                pe.wait_ge(l_x[t // XP], 16)
            if t >= 4:
                pe.wait_ge(s_xt, t - 3)
            for b in range(QB):
                done = nc.tensor.transpose(aux[:, t % 4, b * P:(b + 1) * P], x_nat[:, b, t * P:(t + 1) * P],
                                           ident[:, :])
            done.then_inc(s_tr0, 1)

        def transpose_later(n):
            transpose_x(KU + n)

        def small_inputs():
            pe.wait_ge(s_cp0, 2)
            pe.wait_ge(l_state, 16)
            for t in range(KC):
                nc.tensor.transpose(acc[:, 1, 0, SMALL + t * 2 * DEC:SMALL + (t + 1) * 2 * DEC],
                                    state_nat[:, t * P:(t + 1) * P], ident[0:2 * DEC, 0:2 * DEC])
            pe.wait_ge(l_rows, 16 * 9)
            nc.tensor.transpose(acc[:, 1, 1, SMALL:SMALL + N_ROWS - KT], gain_rows[:, :],
                                ident[0:N_ROWS - KT, 0:N_ROWS - KT])
            pe.wait_ge(l_table, 32)
            for h in range(2):
                done = mm(acc[0:HEADS, 1, h, 0:BIAS_W // 2], rel[:, :],
                          table_sb[:, h * BIAS_W // 2:(h + 1) * BIAS_W // 2], start=True, stop=True)
            done.then_inc(s_tr0, 1)

        pe.wait_ge(s_const, CONSTANTS)
        pe.wait_ge(l_mix, 16)
        nc.tensor.transpose(acc[:, 1, 1, 0:KT], mix_rows[:, :], ident[0:KT, 0:KT]).then_inc(s_tr0, 1)
        pe.wait_ge(l_xs, 16)
        for t in range(KT):
            done = nc.tensor.transpose(acc[:, 1, 0, t * DEC:(t + 1) * DEC], xs_nat[:, t * P:(t + 1) * P],
                                       ident[0:DEC, 0:DEC])
        done.then_inc(s_tr0, 1)
        for t in range(KU):
            transpose_x(t)

        pair(FIRST, 0, None)
        with pe.Fori(0, KA - 1) as a:
            pair(Span(PAIR_UNITS, PAIR_UNITS, a), a + 1, a)

        at = Span(U_CONV)
        for i in range(KT):
            pe.wait_ge(s_read, T_CONV + i - 1)
            unit(at, i, xhi, xlo, range(KC), i % 2, True, True, (s_x, KT + 1) if i == 0 else None)
            if i == 0:
                pe.wait_ge(s_sqs, SQ_CONV)
                pe.wait_ge(s_root, 2 * KA)
                pe.wait_ge(s_natsb, 5 * KA)
                mm(aux[:, BANK_D, 0:HALF], ones[:, :], acc_conv[:, 0:HALF], start=True, stop=True)
                mm(aux[:, BANK_O, 0:HALF], ones[:, :], acc_conv[:, HALF:T], start=True, stop=True).then_inc(s_nsum, 1)
            if i == 1:
                pe.wait_ge(s_nroot, N_CONV)
            if 1 <= i <= PAIR_UNITS:
                attention(KA - 1, i - 1)
            if i == 14:
                pe.wait_ge(s_sqs, SQ_ATTN)
                spread_sum(ones, acc_attn).then_inc(s_nsum, 1)

        with pe.Fori(0, 4) as i:
            at = Span(U_ATTN, 4, i)
            for b in range(4):
                pe.wait_ge(s_read, i * 4 + (T_ATTN + b - 1))
                unit(at, b, xhi, xlo, range(KC, KT), b % 2, True, True, (s_x, KT + KC + 1) if b == 0 else None)

        def transpose_p():
            pe.wait_ge(l_p, 32)
            for t in range(KP):
                for q in range(QB):
                    nc.tensor.transpose(aux[:, BANK_T + t, q * P:(q + 1) * P], p_nat[:, q, t * P:(t + 1) * P],
                                        ident[:, :])
            for t in range(KP):
                done = nc.tensor.transpose(aux[:, BANK_S, t * DEC:(t + 1) * DEC],
                                           ps_nat[:, t * P:(t + 1) * P], ident[0:DEC, 0:DEC])
            done.then_inc(s_ptr, 1)

        def f_tile(at, c, f, fresh=False):
            for n in range(2):
                pe.wait_ge(s_read, f * 2 + (T_FFN + c * CHUNK_TILES + n - 1))
                for part in range(2):
                    unit(at, 2 * n + part, xhi, xlo, range(part * KU, (part + 1) * KU), n, part == 0, part == 1,
                         (s_x, 2 * KT + 1 + part * KU) if fresh and n == 0 else None)
                    if fresh and n == 0 and part == 0:
                        transpose_p()
                    if fresh and n == 1 and part == 0:
                        pe.wait_ge(s_p2, KP)
                        pe.wait_ge(s_sqs, SQ_FFN)
                        spread_sum(ones, acc_h).then_inc(s_nsum, 1)

        for c in range(CHUNKS):
            first = U_FFN + c * CHUNK_UNITS
            if c == 0:
                f_tile(Span(first), 0, 0, fresh=True)
                with pe.Fori(0, CHUNK - 1) as f:
                    f_tile(Span(first + 4, 4, f), c, f + 1)
            else:
                with pe.Fori(0, CHUNK) as f:
                    f_tile(Span(first, 4, f), c, f)
            with pe.Fori(0, KT // 2) as i:
                at = Span(first + 4 * CHUNK, 4, i)
                for b in range(2):
                    pe.wait_ge(s_read, i * 2 + (T_FFN + c * CHUNK_TILES + 2 * CHUNK + b - 1))
                    pe.wait_ge(s_f2, c * CHUNK + DOWN[0])
                    unit(at, b, fhi, flo, range(DOWN[0]), b, True, False)
                for b in range(2):
                    pe.wait_ge(s_f2, (c + 1) * CHUNK)
                    unit(at, 2 + b, fhi, flo, range(DOWN[0], CHUNK), b, False, True)

        at = Span(U_PLE)
        for i in range(KT // PT):
            pe.wait_ge(s_wlo, at.count(i))
            for n in range(PT):
                m = i * PT + n
                if m == 0:
                    pe.wait_ge(s_p2, KP)
                pe.wait_ge(s_read, T_PLE + m - 1)
                for kt in range(KP):
                    at_n = slice((kt * PT + n) * P, (kt * PT + n + 1) * P)
                    for h in range(2):
                        done = products(acc[:, m % 2, h, 0:HALF], whi[:, i % HILO, at_n], wlo[:, i % HILO, at_n],
                                        phi[:, kt, h * HALF:(h + 1) * HALF], plo[:, kt, h * HALF:(h + 1) * HALF],
                                        kt == 0, kt == KP - 1)
                if n < PT - 1:
                    done.then_inc(s_pm, 1)
                else:
                    done.then_inc(s_unit, 1)
        pe.wait_ge(s_x, 4 * KT)
        pe.wait_ge(s_sqs, SQ_PLE)
        spread_sum(ones, acc_h).then_inc(s_nsum, 1)

        def transpose_y(n):
            pe.wait_ge(s_y, n * 2)
            nc.tensor.transpose(aux[0:DEC, BANK_D, 0:P], y_t[:, SEQ:T], ident[:, :])
            for b in range(QB):
                done = nc.tensor.transpose(aux[:, BANK_S, b * P:(b + 1) * P], y_t[:, b * P:(b + 1) * P], ident[:, :])
            done.then_inc(s_ytr, 1)

        def gate(i, first_turn):
            at = Span(U_GATE, 4, i)
            for b in range(2):
                m = i * 2 + b
                pe.wait_ge(s_read, m + (T_GATE - 1))
                for part in range(2):
                    unit(at, 2 * b + part, xhi, xlo, range(part * KU, (part + 1) * KU), b, part == 0, part == 1)
                    if part == 0 and not (first_turn and b == 0):
                        if first_turn:
                            pe.wait_ge(s_nroot, N_PLE)
                        else:
                            pe.wait_ge(s_ycp, (m - 1) * 2)
                        transpose_y(m)

        gate(0, True)
        with pe.Fori(1, KT // 2) as i:
            gate(i, False)
        pe.wait_ge(s_ycp, (KT - 1) * 2)
        transpose_y(KT)

    @block.scalar
    def _(act):
        on = nc.scalar.activation

        def split(at, u):
            act.wait_ge(landed[u % RAW], at.landed(u))
            if not (at.first + u < HILO):
                act.wait_ge(s_unit, at.count(u) - HILO)
            on(whi[:, u % HILO, :], wraw[:, u % RAW, :], ACT.Copy).then_inc(s_whi, 1)

        def root_of(tile, width):
            return on(halves(tile[:, :]), aux_sum, ACT.Sqrt, bias=EPS, scale=1.0 / width)

        def attention(a, g):
            if 1 <= g <= 8:
                c = g - 1
                w = (c % QB + 1) * P
                act.wait_ge(s_pt, 8 * a + (c + 1))
                if c >= 2:
                    act.wait_ge(s_pv, 4 * a + c // 2)
                on(pthi[:, 0:c % QB + 1, c % 2, :], aux[:, BANK_T, 0:w].rearrange("p (k f) -> p k f", f=P), ACT.Copy
                   ).then_inc(s_pthi, 1)
            if g <= 7:
                w = (g % QB + 1) * P
                act.wait_ge(s_nmax, 8 * a + (g + 1))
                on(prob[:, g % 2, 0:w], prob[:, g % 2, 0:w], ACT.Exp, bias=stats[:, 0:1],
                   accum_out=stats[:, 1:2]).then_inc(s_exp, 1)
            if g == 5:
                act.wait_ge(s_row, 5 * a + 2)
                on(row[:, :], row[:, :], ACT.Exp, bias=row_stats[:, 0:1], accum_out=row_stats[:, 1:2]
                   ).then_inc(s_sexp, 1)

        def q_hi(j):
            act.wait_ge(s_qk, 2 * j + 2)
            on(qhi[:, :], q_t[:, 0:SEQ], ACT.Copy).then_inc(s_qkhi, 1)

        def heads(j, a, g, last):
            if g == 7:
                if a is not None:
                    act.wait_ge(s_ssq, 2 * j)
                act.wait_ge(s_read, 6 * j + 3)
                on(sq[:, :], k_t[:, :], ACT.Square).then_inc(s_sq, 1)
            if g == 9:
                act.wait_ge(s_ssq, 2 * j + 1)
                if a is not None:
                    act.wait_ge(s_qk, 2 * j)
                root_of(qk_rstd, HD).then_inc(s_root, 1)
                act.wait_ge(s_read, 6 * j + 3)
                on(sq[:, :], q_t[:, :], ACT.Square).then_inc(s_sq, 1)
                act.wait_ge(s_qk, 2 * j + 1)
                if a is not None:
                    act.wait_ge(s_score, 8 * a + 8)
                on(khi[:, :], k_t[:, 0:SEQ], ACT.Copy).then_inc(s_qkhi, 1)
            if g == 10:
                act.wait_ge(s_ssq, 2 * j + 2)
                root_of(qk_rstd, HD).then_inc(s_root, 1)
                act.wait_ge(s_nat, 2 * j + 1)
                if a is not None:
                    act.wait_ge(d_v, 16 * j)
                    act.wait_ge(d_small, 64 * j)
                on(v_nat[:, :, :], aux[:, BANK_T, :].rearrange("p (b f) -> p b f", b=QB), ACT.Copy).then_inc(s_natsb, 1)
                on(small_nat[0:DEC, 0, :], aux[0:DEC, BANK_O, 0:P], ACT.Copy).then_inc(s_natsb, 1)
                if a is not None:
                    act.wait_ge(s_pv, 4 * a + 4)
                act.wait_ge(s_natsb, 5 * j + 1)
                on(vhi[:, :, :], v_nat[:, :, :], ACT.Copy).then_inc(s_vhi, 1)
                if not last:
                    q_hi(j)
            if g == 11:
                act.wait_ge(s_nat, 2 * j + 2)
                if a is not None:
                    act.wait_ge(d_k, 16 * j)
                on(k_nat[:, :, :], aux[:, BANK_T, :].rearrange("p (b f) -> p b f", b=QB), ACT.Copy).then_inc(s_natsb, 1)
                on(small_nat[0:DEC, 1, :], aux[0:DEC, BANK_O, P:2 * P], ACT.Copy).then_inc(s_natsb, 1)
                on(small_nat[0:DEC + 2, 2, :], aux[0:DEC + 2, BANK_O, 2 * P:3 * P], ACT.Copy).then_inc(s_natsb, 1)

        def pair(at, j, a, last=False):
            for g in range(PAIR_UNITS):
                split(at, g + HILO)
                if a is None and g == 4:
                    act.wait_ge(s_nsum, N_X)
                    root_of(rstd, D_MODEL).then_inc(s_nroot, 1)
                if a is not None:
                    attention(a, g)
                heads(j, a, g, last)
                if last and g == 10:
                    act.wait_ge(s_unit, U_CONV - 1)
                    for c in range(KC - 1):
                        act.wait_ge(s_conv, c + 1)
                        conv_hi(c)

        def conv_hi(c):
            operand_hi(c, hid[:, KA + c, :], ROWS["conv"] + c).then_inc(s_xhi, 1)

        def operand_hi(m, source, gain):
            return on(xhi[:, m, :], source, ACT.Copy, scale=cols[:, bass.ds(gain, 1)])

        act.dma_start(mix_rows[:, :], g_mix[0].rearrange("(t p) -> t p", p=P)).then_inc(l_mix, 16)
        act.dma_start(xs_nat[:, :], x_sample[:, 0, :]).then_inc(l_xs, 16)
        for g in range(1, PIECES):
            at_g = slice(g * XP * P, (g + 1) * XP * P)
            act.dma_start(x_nat[:, :, at_g], x_prompt[0, :, at_g].rearrange("(b p) f -> p b f", p=P)
                          ).then_inc(l_x[g], 16)
        act.wait_ge(s_tr0, 1)
        on(cols[:, 0:KT], acc[:, 1, 1, 0:KT], ACT.Copy).then_inc(s_cp0, 1)
        act.wait_ge(s_tr0, 2)
        on(hid[:, :, SEQ:T], acc[:, 1, 0, 0:KT * DEC].rearrange("p (t b) -> p t b", b=DEC), ACT.Copy).then_inc(s_cp0, 1)

        def square_x(t):
            if t >= 4:
                act.wait_ge(s_sqs, t - 3)
            act.wait_ge(s_xt, t + 1)
            on(tmp[:, t % 4, :], hid[:, t, :], ACT.Square).then_inc(s_xsq, 1)

        for t in range(KT):
            act.wait_ge(s_tr0, t + 3)
            on(hid[:, t, 0:SEQ], aux[:, t % 4, :], ACT.Copy).then_inc(s_xt, 1)
            if t == 0:
                act.wait_ge(s_cp0, 2)
            else:
                square_x(t - 1)
            if t in START_SPLITS:
                split(FIRST, START_SPLITS.index(t))
        square_x(KT - 1)
        act.wait_ge(s_tr0, KT + 3)
        on(cols[:, KT:N_ROWS], acc[:, 1, 1, SMALL:SMALL + N_ROWS - KT], ACT.Copy).then_inc(s_cp0, 1)
        on(state_t[:, :, :], acc[:, 1, 0, SMALL:SMALL + KC * 2 * DEC].rearrange("p (t b) -> p t b", t=KC),
           ACT.Copy).then_inc(s_cp0, 1)
        on(bias_sb.rearrange("h (a w) -> h a w", a=2), acc[0:HEADS, 1, :, 0:BIAS_W // 2], ACT.Copy).then_inc(s_cp0, 1)

        pair(FIRST, 0, None)
        with act.Fori(0, KA - 2) as a:
            pair(Span(PAIR_UNITS, PAIR_UNITS, a), a + 1, a)
        pair(Span((KA - 1) * PAIR_UNITS), KA - 1, KA - 2, last=True)

        at = Span(U_CONV)
        act.wait_ge(s_conv, KC)
        conv_hi(KC - 1)
        q_hi(KA - 1)
        for i in range(KT):
            split(at, i + HILO)
            if i == 0:
                act.wait_ge(s_nsum, N_CONV)
                on(rstd[:, 0:HALF], aux[:, BANK_D, 0:HALF], ACT.Sqrt, bias=EPS, scale=1.0 / D_CONV)
                on(rstd[:, HALF:T], aux[:, BANK_O, 0:HALF], ACT.Sqrt, bias=EPS, scale=1.0 / D_CONV).then_inc(s_nroot, 1)
            if 1 <= i <= PAIR_UNITS:
                attention(KA - 1, i - 1)
            if i < KA - 1:
                operand_hi(KC + i, hid[:, i, :], ROWS["attn"] + i).then_inc(s_xhi, 1)
            if i == 11:
                act.wait_ge(s_o, 2 * KA)
                act.wait_ge(s_out, 4 * KA)
                operand_hi(KT - 1, hid[:, KA - 1, :], ROWS["attn"] + KA - 1).then_inc(s_xhi, 1)
            if i == 14:
                act.wait_ge(s_nsum, N_ATTN)
                root_of(rstd_attn, D_ATTN).then_inc(s_nroot, 1)

        for part in range(2):
            with act.Fori(0, 2) as i:
                at = Span(U_ATTN + 8 * part, 4, i)
                for b in range(4):
                    split(at, b + HILO)
                    if part == 0:
                        m = i * 4 + b
                        act.wait_ge(s_h, i * 4 + (KT + b + 1))
                        operand_hi(m, hid[:, m, :], m + ROWS["ffn"]).then_inc(s_xhi, 1)
        act.wait_ge(s_unit, U_FFN)
        act.wait_ge(s_h, 2 * KT)
        for m in range(KT // 2, KT):
            operand_hi(m, hid[:, m, :], ROWS["ffn"] + m).then_inc(s_xhi, 1)

        def f_tile(at, c, f, fresh=False):
            n = f + c * CHUNK
            split(at, HILO)
            split(at, HILO + 1)
            if fresh:
                act.wait_ge(s_ptr, 1)
                for t in range(KP):
                    on(phi[:, t, 0:SEQ], aux[:, BANK_T + t, :], ACT.Copy)
                    on(phi[:, t, SEQ:T], aux[:, BANK_S, t * DEC:(t + 1) * DEC], ACT.Copy).then_inc(s_phi, 1)
                act.wait_ge(s_nsum, N_FFN)
                root_of(rstd, D_MODEL).then_inc(s_nroot, 1)
            act.wait_ge(s_read, f * 2 + (T_FFN + c * CHUNK_TILES + 1))
            on(act_t[:, :], res[:, 0, :], ACT.Sigmoid).then_inc(s_sig, 1)
            split(at, HILO + 2)
            act.wait_ge(s_f, n * 2 + 2)
            on(fhi[:, f, :], res[:, 0, :], ACT.Copy).then_inc(s_fhi, 1)
            split(at, HILO + 3)

        for c in range(CHUNKS):
            first = U_FFN + c * CHUNK_UNITS
            if c == 0:
                f_tile(Span(first), 0, 0, fresh=True)
                with act.Fori(0, CHUNK - 1) as f:
                    f_tile(Span(first + 4, 4, f), c, f + 1)
            else:
                with act.Fori(0, CHUNK) as f:
                    f_tile(Span(first, 4, f), c, f)
            with act.Fori(0, KT // 2) as i:
                at = Span(first + 4 * CHUNK, 4, i)
                split(at, HILO)
                split(at, HILO + 1)
                for b in range(2):
                    split(at, HILO + 2 + b)
                    if c == CHUNKS - 1:
                        m = i * 2 + b
                        act.wait_ge(s_read, i * 2 + (T_PLE - KT + b + 1))
                        operand_hi(m, hid[:, m, :], m + ROWS["ple"]).then_inc(s_xhi, 1)

        for u in range(KT // PT):
            split(Span(U_PLE), u + HILO)
        act.wait_ge(s_nsum, N_PLE)
        root_of(rstd, D_MODEL).then_inc(s_nroot, 1)

        def copy_y(n, slot):
            act.wait_ge(s_ytr, n)
            on(y_nat[:, slot, :, :], aux[:, BANK_S, :].rearrange("p (b f) -> p b f", b=QB), ACT.Copy).then_inc(s_ycp, 1)
            on(ys_nat[:, slot, :], aux[0:DEC, BANK_D, 0:P], ACT.Copy).then_inc(s_ycp, 1)

        def gate(i, stored, last_turn=False):
            at = Span(U_GATE, 4, i)
            for b in range(2):
                m = i * 2 + b
                if not last_turn:
                    split(at, HILO + 2 * b)
                if b == 0 and stored != "none":
                    if stored == "both":
                        act.wait_ge(d_y[1], i * 32 - 32)
                    copy_y(m, 1)
                if b == 1:
                    if stored != "none":
                        act.wait_ge(d_y[0], i * 32)
                    copy_y(m, 0)
                act.wait_ge(s_read, m + (T_GATE + 1))
                on(act_t[:, :], res[:, 0, :], ACT.Sigmoid).then_inc(s_sig, 1)
                if not last_turn:
                    split(at, HILO + 2 * b + 1)

        gate(0, "none")
        gate(1, "slot 0")
        with act.Fori(2, KT // 2 - 1) as i:
            gate(i, "both")
        gate(KT // 2 - 1, "both", last_turn=True)
        act.wait_ge(d_y[1], (KT // 2 - 1) * 32)
        copy_y(KT, 1)

    @block.vector
    def _(dve):
        V = nc.vector

        def split(at, u):
            dve.wait_ge(s_whi, at.count(u))
            V.tensor_tensor(wlo[:, u % HILO, :], wraw[:, u % RAW, :], whi[:, u % HILO, :].bitcast(F32),
                            ALU.subtract).then_inc(s_wlo, 1)

        def scaled(out, slot, by):
            return V.tensor_tensor(halves(out), acc_of(slot), halves(by[:, :]), ALU.mult)

        def operand_lo(m, source, gain):
            return V.scalar_tensor_tensor(xlo[:, m, :], source, cols[:, bass.ds(gain, 1)],
                                          xhi[:, m, :].bitcast(F32), ALU.mult, ALU.subtract)

        def attention(a, g):
            if 1 <= g <= 8:
                c = g - 1
                w = (c % QB + 1) * P
                dve.wait_ge(s_pthi, 8 * a + (c + 1))
                V.tensor_tensor(ptlo[:, 0:c % QB + 1, c % 2, :], aux[:, BANK_T, 0:w].rearrange("p (k f) -> p k f", f=P),
                                pthi[:, 0:c % QB + 1, c % 2, :].bitcast(F32), ALU.subtract).then_inc(s_pt2, 1)
            if g == 5 or g == 9:
                e = (g - 5) // 4
                dve.wait_ge(s_pv, 4 * a + 2 * (e + 1))
                V.tensor_copy(hid[e * HD:(e + 1) * HD, a, 0:SEQ], aux[e * HD:(e + 1) * HD, BANK_O, :]).then_inc(s_o, 1)
            if g <= 7:
                e, w = g // QB, (g % QB + 1) * P
                buf = prob[:, g % 2, 0:w]
                if g == 0:
                    dve.wait_ge(l_skew, 16 * a + 16)
                if g >= 2:
                    dve.wait_ge(s_pt, 8 * a + (g - 1))
                dve.wait_ge(s_score, 8 * a + (g + 1))
                V.scalar_tensor_tensor(buf, aux[:, BANK_S, 0:w], HD ** -0.5, skew[:, e, SEQ - w:SEQ],
                                       ALU.mult, ALU.add).then_inc(s_biased, 1)
                dve.wait_ge(s_biased, 8 * a + (g + 1))
                V.tensor_reduce(stats[:, 0:1], buf, X, ALU.max, negate=True).then_inc(s_nmax, 1)
            if g <= 7:
                buf = prob[:, g % 2, 0:(g % QB + 1) * P]
                dve.wait_ge(s_exp, 8 * a + (g + 1))
                V.reciprocal(stats[:, 2:3], stats[:, 1:2]).then_inc(s_rden, 1)
                dve.wait_ge(s_rden, 8 * a + (g + 1))
                V.tensor_scalar(buf, buf, stats[:, 2:3], None, ALU.mult).then_inc(s_prob, 1)
            if g == 1:
                dve.wait_ge(s_qb, 2 * a + 1)
                dve.wait_ge(l_kc, 16 * a + 16)
                keys_times_q(0).then_inc(s_mul, 1)
            if g == 2:
                dve.wait_ge(s_qb, 2 * a + 2)
                keys_times_q(1).then_inc(s_mul, 1)
            if g == 3:
                dve.wait_ge(s_mul, 2 * a + 2)
                for t in range(KCACHE):
                    V.tensor_reduce(key_sc[:, t, :].rearrange("p (b e) -> p b e", b=DEC),
                                    kv.rearrange("p (b t) (e d) -> p b t e d", t=KCACHE, e=2)[:, :, t, :, :],
                                    X, ALU.add).then_inc(s_key, 1)
                V.tensor_tensor(kq_s[:, :], qkv_s[:, 0, :], qkv_s[:, 1, :], ALU.mult).then_inc(s_key, 1)
                dve.wait_ge(s_key, 4 * a + 3)
                V.tensor_tensor(kq_pair[:, :, :], kq_s[:, :].unsqueeze(2).broadcast_to([P, DEC, 2]),
                                half_mask[:, :].unsqueeze(1).broadcast_to([P, DEC, 2]), ALU.mult).then_inc(s_key, 1)
            if g == 5:
                dve.wait_ge(l_row, 16 * a + 16)
                dve.wait_ge(s_str, 2 * a + 1)
                V.scalar_tensor_tensor(row[:, :], aux[0:2 * DEC, BANK_D, 0:ROW_W], HD ** -0.5, row_bias[:, :],
                                       ALU.mult, ALU.add).then_inc(s_row, 1)
                dve.wait_ge(s_row, 5 * a + 1)
                V.tensor_reduce(row_stats[:, 0:1], row[:, :], X, ALU.max, negate=True).then_inc(s_row, 1)
            if g == 6:
                dve.wait_ge(s_sexp, a + 1)
                V.reciprocal(row_stats[:, 2:3], row_stats[:, 1:2]).then_inc(s_row, 1)
                dve.wait_ge(s_row, 5 * a + 3)
                V.tensor_scalar(row[:, :], row[:, :], row_stats[:, 2:3], None, ALU.mult).then_inc(s_row, 1)
                dve.wait_ge(s_row, 5 * a + 4)
                V.tensor_scalar(new_diag[:, :], ident[0:2 * DEC, 0:2 * DEC], row[:, PAST:PAST + 1], None,
                                ALU.mult).then_inc(s_row, 1)
            if g == 7:
                dve.wait_ge(s_str, 2 * a + 2)
                V.tensor_copy(p_cols.rearrange("p t c -> p (t c)"), aux[:, BANK_D, 0:3 * 2 * DEC]).then_inc(s_pc, 1)
            if g == 8:
                dve.wait_ge(s_pc, a + 1)
                V.tensor_tensor(out_s[:, :, :], qkv_s[:, 2, :].unsqueeze(2).broadcast_to([P, DEC, 2]),
                                p_cols[:, KCACHE, :].rearrange("p (b e) -> p b e", b=DEC), ALU.mult).then_inc(s_out, 1)
                dve.wait_ge(s_out, 4 * a + 1)
                dve.wait_ge(s_spv, a + 1)
                V.tensor_tensor(out_s[:, :, :], out_s[:, :, :],
                                aux[:, BANK_D, 0:2 * DEC].rearrange("p (b e) -> p b e", b=DEC),
                                ALU.add).then_inc(s_out, 1)
                dve.wait_ge(s_out, 4 * a + 2)
                for e in range(2):
                    V.tensor_copy(hid[e * HD:(e + 1) * HD, a, SEQ:T], out_s[e * HD:(e + 1) * HD, :, e]
                                  ).then_inc(s_out, 1)

        def keys_times_q(e):
            part = kv.rearrange("p (b t) f -> p b t f", t=KCACHE)[:, 4 * e:4 * e + 4, :, :]
            return V.tensor_tensor(part, part, aux[:, BANK_D, :].rearrange("p (b f) -> p b f", b=4)
                                   .unsqueeze(2).broadcast_to([P, 4, KCACHE, P]), ALU.mult)

        def norm_q(j):
            norm_head(q_t, ROWS["q"], 2 * j + 1)
            V.tensor_copy(qkv_s[:, 0, :], q_t[:, SEQ:T]).then_inc(s_cols, 1)
            V.tensor_copy(qkv_s[:, 2, :], v_t[:, SEQ:T]).then_inc(s_cols, 1)
            dve.wait_ge(s_vhi, j + 1)
            V.tensor_tensor(vlo[:, :, :], v_nat[:, :, :], vhi[:, :, :].bitcast(F32), ALU.subtract).then_inc(s_v2, 1)
            dve.wait_ge(s_qkhi, 2 * j + 2)
            V.tensor_tensor(qlo[:, :], q_t[:, 0:SEQ], qhi[:, :].bitcast(F32), ALU.subtract).then_inc(s_qk2, 1)

        def heads(j, a, g, last):
            if a is None and g == 5:
                dve.wait_ge(d_bias, 16)
                V.memset(u_t[:, 0:2], 0.0).then_inc(s_pad, 1)
                dve.wait_ge(s_nroot, N_X)
                V.reciprocal(rstd[:, :], rstd[:, :]).then_inc(s_ninv, 1)
                dve.wait_ge(s_ninv, N_X)
                dve.wait_ge(s_read, 2)
                for tile in (v_t, k_t):
                    V.tensor_tensor(tile[:, :], tile[:, :], rstd[:, :], ALU.mult)
            if g == 1:
                dve.wait_ge(s_unit, 12 * j + 2)
                if a is None:
                    V.tensor_copy(halves(v_t[:, :]), acc_of(0)).then_inc(s_read, 1)
                else:
                    scaled(v_t[:, :], 0, rstd).then_inc(s_read, 1)
            if g == 3:
                dve.wait_ge(s_unit, 12 * j + 4)
                if a is None:
                    V.tensor_copy(halves(k_t[:, :]), acc_of(1)).then_inc(s_read, 1)
                else:
                    dve.wait_ge(s_nat, 2 * j)
                    scaled(k_t[:, :], 1, rstd).then_inc(s_read, 1)
            if g == 5:
                dve.wait_ge(s_unit, 12 * j + 6)
                if a is not None:
                    dve.wait_ge(s_qkhi, 2 * j)
                scaled(q_t[:, :], 0, rstd).then_inc(s_read, 1)
            if g == 7:
                dve.wait_ge(s_unit, 12 * j + 8)
                if a is not None:
                    dve.wait_ge(s_conv, j)
                scaled(conv[:, :], 1, rstd).then_inc(s_read, 1)
            if g == 9:
                dve.wait_ge(s_unit, 12 * j + 10)
                scaled(gate_t[:, :], 0, rstd).then_inc(s_read, 1)
                dve.wait_ge(s_read, 6 * j + 5)
                V.tensor_tensor(u_t[:, 2:2 + T], conv[:, :], gate_t[:, :], ALU.mult).then_inc(s_u, 1)
                norm_head(k_t, ROWS["k"], 2 * j)
                V.tensor_copy(qkv_s[:, 1, :], k_t[:, SEQ:T]).then_inc(s_cols, 1)
                dve.wait_ge(s_qkhi, 2 * j + 1)
                V.tensor_tensor(klo[:, :], k_t[:, 0:SEQ], khi[:, :].bitcast(F32), ALU.subtract).then_inc(s_qk2, 1)
            if g == 10:
                def tap(t):
                    return cols[:, bass.ds(j + (ROWS["taps"] + t * KC), 1)]

                old = state_t[:, j, :].rearrange("p (b t) -> p b t", t=2)
                if a is None:
                    dve.wait_ge(s_pad, 1)
                dve.wait_ge(s_u, j + 1)
                V.tensor_scalar(conv[:, :], u_t[:, 2:2 + T], tap(2), None, ALU.mult).then_inc(s_tap, 1)
                for n, t in enumerate((1, 0)):
                    dve.wait_ge(s_tap, 5 * j + (2 * n + 1))
                    V.scalar_tensor_tensor(conv[:, 0:SEQ], u_t[:, t:t + SEQ], tap(t), conv[:, 0:SEQ],
                                           ALU.mult, ALU.add).then_inc(s_tap, 1)
                    V.scalar_tensor_tensor(conv[:, SEQ:T], old[:, :, t], tap(t), conv[:, SEQ:T],
                                           ALU.mult, ALU.add).then_inc(s_tap, 1)
                if not last:
                    norm_q(j)
            if g == 11:
                dve.wait_ge(s_unit, 12 * j + 12)
                scaled(gate_t[:, :], 1, rstd).then_inc(s_read, 1)
                dve.wait_ge(s_read, 6 * j + 6)
                dve.wait_ge(s_tap, 5 * j + 5)
                if a is None:
                    dve.wait_ge(d_spill, 64)
                V.tensor_tensor(hid[:, j + KA, :], conv[:, :], gate_t[:, :], ALU.mult).then_inc(s_conv, 1)

        def norm_head(tile, gain, n):
            dve.wait_ge(s_root, n + 1)
            V.reciprocal(qk_rstd[:, :], qk_rstd[:, :]).then_inc(s_inv, 1)
            dve.wait_ge(s_inv, n + 1)
            V.scalar_tensor_tensor(tile[:, :], tile[:, :], cols[:, gain:gain + 1], qk_rstd[:, :],
                                   ALU.mult, ALU.mult).then_inc(s_qk, 1)
            dve.wait_ge(s_qk, n + 1)

        def pair(at, j, a, last=False):
            for g in range(PAIR_UNITS):
                split(at, g + HILO)
                if a is not None:
                    attention(a, g)
                heads(j, a, g, last)
                if last and g == 10:
                    for c in range(KC - 1):
                        conv_lo(c)

        def conv_lo(c):
            dve.wait_ge(s_xhi, KT + c + 1)
            operand_lo(c, hid[:, KA + c, :], ROWS["conv"] + c).then_inc(s_x, 1)

        V.memset(ones[:, :], 1.0).then_inc(s_const, 1)
        V.memset(rel[BUCKETS:BUCKETS + 1, :], 1.0).then_inc(s_const, 1)
        V.memset(acc_conv, 0.0).then_inc(s_const, 1)
        V.memset(acc_attn, 0.0).then_inc(s_const, 1)
        for e in range(2):
            for d in range(2):
                V.memset(headsum[e * HD:(e + 1) * HD, d * HD:(d + 1) * HD], float(e == d)).then_inc(s_const, 1)
                V.memset(half_mask[e * HD:(e + 1) * HD, d:d + 1], float(e == d)).then_inc(s_const, 1)
        for t in range(KT):
            if t == 0:
                dve.wait_ge(s_cp0, 2)
            dve.wait_ge(s_xt, t + 1)
            gain = cols[:, ROWS["mix"] + t:ROWS["mix"] + t + 1]
            V.tensor_scalar(xhi[:, t, :], hid[:, t, :], gain, None, ALU.mult).then_inc(s_xhi, 1)
            dve.wait_ge(s_xhi, t + 1)
            operand_lo(t, hid[:, t, :], ROWS["mix"] + t).then_inc(s_x, 1)
            if t in START_SPLITS:
                split(FIRST, START_SPLITS.index(t))
        dve.wait_ge(s_const, CONSTANTS)
        pair(FIRST, 0, None)
        with dve.Fori(0, KA - 2) as a:
            pair(Span(PAIR_UNITS, PAIR_UNITS, a), a + 1, a)
        pair(Span((KA - 1) * PAIR_UNITS), KA - 1, KA - 2, last=True)

        at = Span(U_CONV)
        conv_lo(KC - 1)
        norm_q(KA - 1)
        for i in range(KT):
            m = (KA + i) % KT
            split(at, i + HILO)
            if i == 0:
                dve.wait_ge(s_nroot, N_CONV)
                V.reciprocal(rstd[:, :], rstd[:, :]).then_inc(s_ninv, 1)
                dve.wait_ge(s_ninv, N_CONV)
            dve.wait_ge(s_unit, U_CONV + i + 1)
            if i > 0:
                dve.wait_ge(s_h, i)
            scaled(act_t[:, :], i % 2, rstd).then_inc(s_read, 1)
            dve.wait_ge(s_read, T_CONV + i + 1)
            dve.wait_ge(l_res[i % 2], 16 * (i // 2 + 1))
            V.tensor_tensor(hid[:, m, :], act_t[:, :], res[:, i % 2, :], ALU.add).then_inc(s_h, 1)
            if 1 <= i <= PAIR_UNITS:
                attention(KA - 1, i - 1)
            if i < KA - 1 or i == 11:
                t = min(i, KA - 1)
                dve.wait_ge(s_xhi, KT + KC + t + 1)
                operand_lo(KC + t, hid[:, t, :], ROWS["attn"] + t).then_inc(s_x, 1)
            if i == KT - 1:
                dve.wait_ge(s_nroot, N_ATTN)
                V.reciprocal(rstd_attn[:, :], rstd_attn[:, :]).then_inc(s_ninv, 1)

        dve.wait_ge(s_ninv, N_ATTN)
        for part in range(2):
            with dve.Fori(0, 2) as i:
                at = Span(U_ATTN + 8 * part, 4, i)
                for b in range(4):
                    m = i * 4 + (8 * part + b)
                    split(at, b + HILO)
                    dve.wait_ge(s_unit, m + (U_ATTN + 1))
                    dve.wait_ge(s_h, m + KT)
                    scaled(act_t[:, :], b % 2, rstd_attn).then_inc(s_read, 1)
                    dve.wait_ge(s_read, m + (T_ATTN + 1))
                    V.tensor_tensor(hid[:, m, :], act_t[:, :], hid[:, m, :], ALU.add).then_inc(s_h, 1)
                    if part == 0:
                        dve.wait_ge(s_xhi, m + (2 * KT + 1))
                        operand_lo(m, hid[:, m, :], m + ROWS["ffn"]).then_inc(s_x, 1)
        for m in range(KT // 2, KT):
            dve.wait_ge(s_xhi, 2 * KT + m + 1)
            operand_lo(m, hid[:, m, :], ROWS["ffn"] + m).then_inc(s_x, 1)

        def f_tile(at, c, f, fresh=False):
            n = f + c * CHUNK
            split(at, HILO)
            split(at, HILO + 1)
            if fresh:
                dve.wait_ge(s_phi, KP)
                for t in range(KP):
                    V.tensor_tensor(plo[:, t, 0:SEQ], aux[:, BANK_T + t, :], phi[:, t, 0:SEQ].bitcast(F32),
                                    ALU.subtract)
                    V.tensor_tensor(plo[:, t, SEQ:T], aux[:, BANK_S, t * DEC:(t + 1) * DEC],
                                    phi[:, t, SEQ:T].bitcast(F32), ALU.subtract).then_inc(s_p2, 1)
                dve.wait_ge(s_nroot, N_FFN)
                V.reciprocal(rstd[:, :], rstd[:, :]).then_inc(s_ninv, 1)
                dve.wait_ge(s_ninv, N_FFN)
            else:
                dve.wait_ge(s_f2, n)
            dve.wait_ge(s_unit, at.count(1))
            scaled(res[:, 0, :], 0, rstd).then_inc(s_read, 1)
            split(at, HILO + 2)
            dve.wait_ge(s_unit, at.count(3))
            scaled(res[:, 1, :], 1, rstd).then_inc(s_read, 1)
            dve.wait_ge(s_sig, n + 1)
            V.tensor_tensor(res[:, 0, :], res[:, 0, :], act_t[:, :], ALU.mult).then_inc(s_f, 1)
            dve.wait_ge(s_f, n * 2 + 1)
            dve.wait_ge(s_read, f * 2 + (T_FFN + c * CHUNK_TILES + 2))
            V.tensor_tensor(res[:, 0, :], res[:, 0, :], res[:, 1, :], ALU.mult).then_inc(s_f, 1)
            dve.wait_ge(s_fhi, n + 1)
            V.tensor_tensor(flo[:, f, :], res[:, 0, :], fhi[:, f, :].bitcast(F32), ALU.subtract).then_inc(s_f2, 1)
            split(at, HILO + 3)

        for c in range(CHUNKS):
            first = U_FFN + c * CHUNK_UNITS
            if c == 0:
                f_tile(Span(first), 0, 0, fresh=True)
                with dve.Fori(0, CHUNK - 1) as f:
                    f_tile(Span(first + 4, 4, f), c, f + 1)
            else:
                with dve.Fori(0, CHUNK) as f:
                    f_tile(Span(first, 4, f), c, f)
            with dve.Fori(0, KT // 2) as i:
                at = Span(first + 4 * CHUNK, 4, i)
                split(at, HILO)
                split(at, HILO + 1)
                for b in range(2):
                    m = i * 2 + b
                    dve.wait_ge(s_unit, at.count(2 + b))
                    V.tensor_tensor(halves(hid[:, m, :]), acc_of(b), halves(hid[:, m, :]), ALU.add).then_inc(s_read, 1)
                    split(at, HILO + 2 + b)
                    if c == CHUNKS - 1:
                        dve.wait_ge(s_xhi, m + (3 * KT + 1))
                        operand_lo(m, hid[:, m, :], m + ROWS["ple"]).then_inc(s_x, 1)

        for u in range(KT // PT):
            for n in range(PT):
                if n == PT - 1:
                    dve.wait_ge(s_unit, U_PLE + u + 1)
                else:
                    dve.wait_ge(s_pm, u * (PT - 1) + n + 1)
                m = u * PT + n
                V.tensor_copy(halves(proj[:, m, :]), acc_of(m % 2)).then_inc(s_read, 1)
            split(Span(U_PLE), u + HILO)
        dve.wait_ge(s_nroot, N_PLE)
        V.reciprocal(rstd[:, :], rstd[:, :]).then_inc(s_ninv, 1)
        dve.wait_ge(s_ninv, N_PLE)

        def gate(i, first_turn=False, last_turn=False):
            at = Span(U_GATE, 4, i)
            for b in range(2):
                m = i * 2 + b
                if not last_turn:
                    split(at, HILO + 2 * b)
                dve.wait_ge(s_unit, at.count(2 * b + 1))
                scaled(res[:, 0, :], b, rstd).then_inc(s_read, 1)
                dve.wait_ge(s_sig, m + (CHUNKS * CHUNK + 1))
                if not (first_turn and b == 0):
                    dve.wait_ge(s_y, m * 2)
                V.tensor_tensor(res[:, 1, :], proj[:, m, :], act_t[:, :], ALU.mult).then_inc(s_y, 1)
                dve.wait_ge(s_y, m * 2 + 1)
                if not (first_turn and b == 0):
                    dve.wait_ge(s_ytr, m)
                V.tensor_tensor(y_t[:, :], res[:, 1, :], hid[:, m, :], ALU.add).then_inc(s_y, 1)
                if not last_turn:
                    split(at, HILO + 2 * b + 1)

        gate(0, first_turn=True)
        with dve.Fori(1, KT // 2 - 1) as i:
            gate(i)
        gate(KT // 2 - 1, last_turn=True)

    @block.gpsimd
    def _(pool):
        G = nc.gpsimd

        def apart():
            pool.sem_inc(s_passed, 1)

        def add_squares(total, tile, before):
            pool.wait_ge(s_sqs, before)
            G.tensor_tensor(gsq[:, :], tile, tile, ALU.mult).then_inc(s_sqs, 1)
            pool.wait_ge(s_sqs, before + 1)
            G.tensor_tensor(total, total, gsq[:, :], ALU.add).then_inc(s_sqs, 1)

        def load_keys(a):
            pool.dma_start(kv[:, :, :], cache_k[0].rearrange("b (t p) h d -> p (b t) (h d)", p=P)[
                :, :, bass.ts(a, P)]).then_inc(l_kc, 16)

        def load_bias(a):
            pool.dma_start(row_bias[:, :], row_dram[a].rearrange("b e i -> (b e) i")).then_inc(l_row, 16)

        def load_skew(a):
            pool.dma_start(skew[:, :, :], skew_dram[bass.ds(a * 2, 2)].rearrange("e p y -> p e y")).then_inc(l_skew, 16)

        def load_values(a):
            pool.wait_ge(s_key, 4 * a + 2)
            apart()
            pool.dma_start(kv[:, :, :], cache_v[0].rearrange("b (t p) h d -> p (b t) (h d)", p=P)[
                :, :, bass.ts(a, P)]).then_inc(l_vc, 16)

        def attention(a):
            load_values(a)
            pool.wait_ge(s_row, 5 * a + 1)
            apart()
            load_bias(a + 1)
            pool.wait_ge(s_spv, a + 1)
            apart()
            load_keys(a + 1)
            pool.wait_ge(s_biased, 8 * a + 8)
            apart()
            load_skew(a + 1)
            pool.wait_ge(s_o, 2 * a + 2)
            pool.wait_ge(s_out, 4 * a + 4)
            add_squares(acc_attn, hid[:, a, :], 4 * a + (SQ_X + 2))

        def store_rows(j):
            at = bass.ts(j, P)
            pool.wait_ge(s_natsb, 5 * j + 1)
            apart()
            pool.dma_start(v_prompt[0, 0].rearrange("(b p) h d -> p b (h d)", p=P)[:, :, at], v_nat[:, :, :]
                           ).then_inc(d_v, 16)
            pool.wait_ge(s_natsb, 5 * j + 3)
            apart()
            pool.dma_start(k_prompt[0, 0].rearrange("(b p) h d -> p b (h d)", p=P)[:, :, at], k_nat[:, :, :]
                           ).then_inc(d_k, 16)
            pool.wait_ge(s_natsb, 5 * j + 5)
            apart()
            pool.dma_start(v_sample[0, :, 0].rearrange("b h d -> b (h d)")[:, at], small_nat[0:DEC, 0, :]
                           ).then_inc(d_small, 16)
            pool.dma_start(k_sample[0, :, 0].rearrange("b h d -> b (h d)")[:, at], small_nat[0:DEC, 1, :]
                           ).then_inc(d_small, 16)
            pool.dma_start(conv_prompt[0, 0][:, at], small_nat[0:2, 2, :]).then_inc(d_small, 16)
            pool.dma_start(conv_sample[0, :, 1, at], small_nat[2:DEC + 2, 2, :]).then_inc(d_small, 16)

        G.memset(ident[:, :], 0.0).then_inc(s_ident, 1)
        pool.wait_ge(s_ident, 1)
        G.affine_select(out=ident[:, :], in_=ident[:, :], compare_op=ALU.not_equal, fill=1.0, base=0,
                        pattern=[[-1, P]], channel_multiplier=1).then_inc(s_const, 1)

        def gains(name, count, source):
            first = ROWS[name] - KT
            pool.dma_start(gain_rows[first:first + count, :], source).then_inc(l_rows, 16)

        gains("ffn", KT, g_ffn[0].rearrange("(t p) -> t p", p=P))
        gains("ple", KT, g_ple[0].rearrange("(t p) -> t p", p=P))
        gains("attn", KA, g_attn_out[0].rearrange("(t p) -> t p", p=P))
        gains("conv", KC, g_conv_out[0].rearrange("(t p) -> t p", p=P))
        gains("taps", 3 * KC, conv_w[0].rearrange("c (t p) -> (c t) p", p=P))
        for name, norm in (("q", q_norm), ("k", k_norm)):
            for e in range(2):
                pool.dma_start(gain_rows[ROWS[name] - KT:ROWS[name] - KT + 1, e * HD:(e + 1) * HD], norm
                               ).then_inc(l_rows, 16)
        pool.dma_start(state_nat[:, :], state_conv[0].rearrange("b t c -> (b t) c")).then_inc(l_state, 16)
        pool.dma_start(rel[0:BUCKETS, :], rel_bias).then_inc(l_table, 16)
        pool.dma_start(table_sb[:, :], table).then_inc(l_table, 16)
        for t in range(KT):
            pool.wait_ge(s_xsq, t + 1)
            if t > 0:
                pool.wait_ge(s_sqs, t)
            else:
                pool.wait_ge(s_const, CONSTANTS)
            G.tensor_tensor(acc_attn, acc_attn, tmp[:, t % 4, :], ALU.add).then_inc(s_sqs, 1)
        pool.wait_ge(s_cp0, 5)
        pool.dma_start(bias_dram, bias_sb[:, :]).then_inc(d_bias, 16)
        pool.wait_ge(d_bias, 16)

        def store_skew(first, last):
            shifted = bias_dram[first:last, P - 1:P - 1 + SEQ]
            shifted = bass.AP(tensor=shifted.tensor, offset=shifted.offset,
                              ap=[[BIAS_W, last - first], [-1, P], [1, SEQ]])
            pool.dma_start(skew_dram[first:last], shifted).then_inc(d_skew, 16)

        store_skew(0, 2)
        for e in range(2):
            rows = bias_dram[e:HEADS:2, PAST - 1:PAST - 1 + ROW_W]
            pool.dma_start(row_dram[:, :, e, :], rows.unsqueeze(1).broadcast_to([KA, DEC, ROW_W])).then_inc(d_rows, 16)
        load_keys(0)
        pool.wait_ge(d_rows, 32)
        load_bias(0)
        pool.wait_ge(d_skew, 16)
        load_skew(0)
        pool.wait_ge(s_nsum, N_X)
        G.memset(acc_attn, 0.0).then_inc(s_zero, 1)
        pool.wait_ge(s_zero, 1)
        pool.wait_ge(s_xt, KT)
        for n in range(4):
            pool.wait_ge(s_unit, 4 + n)
            pool.dma_start(xt_dram[:, n * 4:(n + 1) * 4, :], hid[:, n * 4:(n + 1) * 4, :]).then_inc(d_spill, 16)
        for n in range(1, KA):
            pool.wait_ge(s_unit, 7 + min(n, 4))
            store_skew(2 * n, 2 * n + 2)
        pool.dma_start(conv_sample[0, :, 0, :], state_conv[0, :, 1, :]).then_inc(d_state, 16)

        store_rows(0)
        pool.wait_ge(s_conv, 1)
        add_squares(acc_conv, hid[:, KA, :], SQ_X)
        pool.wait_ge(d_skew, 16 * KA)
        with pool.Fori(0, KA - 1) as a:
            attention(a)
            store_rows(a + 1)
            pool.wait_ge(s_conv, a + 2)
            add_squares(acc_conv, hid[:, a + (KA + 1), :], 4 * a + (SQ_X + 4))

        for i in range(KT):
            if i < 2:
                pool.wait_ge(s_conv, KC)
            else:
                pool.wait_ge(s_h, i - 1)
            pool.dma_start(res[:, i % 2, :], xt_dram[:, (KA + i) % KT, :]).then_inc(l_res[i % 2], 16)
            if i == 6:
                load_values(KA - 1)
            if i == 12:
                pool.wait_ge(s_o, 2 * KA)
                pool.wait_ge(s_out, 4 * KA)
                add_squares(acc_attn, hid[:, KA - 1, :], SQ_CONV)

        G.memset(acc_h, 0.0).then_inc(s_zero, 1)
        pool.wait_ge(s_zero, 2)
        pool.wait_ge(d_v, 16 * KA)
        pool.wait_ge(d_k, 16 * KA)
        pool.wait_ge(d_small, 64 * KA)
        pool.dma_start(p_nat[:, :, :], p_prompt[0, 0].rearrange("(b p) f -> p b f", p=P)).then_inc(l_p, 16)
        pool.dma_start(ps_nat[:, :], p_sample[0, :, 0, :]).then_inc(l_p, 16)
        with pool.Fori(0, KT) as m:
            pool.wait_ge(s_h, m + (KT + 1))
            add_squares(acc_h, hid[:, m, :], m * 2 + SQ_ATTN)

        pool.wait_ge(s_nsum, N_FFN)
        G.memset(acc_h, 0.0).then_inc(s_zero, 1)
        pool.wait_ge(s_zero, 3)
        with pool.Fori(0, KT) as m:
            pool.wait_ge(s_read, m + (T_PLE - KT + 1))
            add_squares(acc_h, hid[:, m, :], m * 2 + SQ_FFN)

        with pool.Fori(0, KT // 2) as i:
            for b in range(2):
                m = i * 2 + b
                pool.wait_ge(s_ycp, i * 4 + (2 * b + 2))
                apart()
                pool.dma_start(y_prompt[0].rearrange("(b p) f -> p b f", p=P)[:, :, bass.ts(m, P)],
                               y_nat[:, b, :, :]).then_inc(d_y[b], 16)
                pool.dma_start(y_sample[:, 0, bass.ts(m, P)], ys_nat[:, b, :]).then_inc(d_y[b], 16)
        for b in range(2):
            pool.wait_ge(d_y[b], KT // 2 * 32)
        pool.wait_ge(d_state, 16)
        pool.wait_ge(d_spill, 64)

    ctx.close()


def kernel(**inputs):
    import concourse.bacc as bacc
    from concourse.bass_utils import run_bass_kernel_spmd as run

    nc = bacc.Bacc("TRN2", target_bir_lowering=False, num_devices=1)
    names = ("x_prompt", "x_sample", "p_prompt", "p_sample", "cache_k", "cache_v", "state_conv", "rel_bias",
             "g_mix", "w_in", "q_norm", "k_norm", "conv_w", "g_attn_out", "g_conv_out", "w_out", "g_ffn",
             "w_gate", "w_up", "w_down", "g_ple", "w_ple_gate", "w_ple_proj")
    arrays = {f"in_{n}": np.ascontiguousarray(inputs[n]) for n in names}
    arrays["in_table"] = bucket_table()
    args = [nc.dram_tensor(n, a.shape, mybir.dt.from_np(a.dtype), kind="ExternalInput").ap()
            for n, a in arrays.items()]
    outs = dict(y_prompt=(1, SEQ, D_MODEL), y_sample=(DEC, 1, D_MODEL), k_prompt=(1, 1, SEQ, HEADS, HD),
                v_prompt=(1, 1, SEQ, HEADS, HD), conv_prompt=(1, 1, 2, D_CONV), k_sample=(1, DEC, 1, HEADS, HD),
                v_sample=(1, DEC, 1, HEADS, HD), conv_sample=(1, DEC, 2, D_CONV))
    args += [nc.dram_tensor(f"out_{n}", s, F32, kind="ExternalOutput").ap() for n, s in outs.items()]
    build(nc, *args)
    got = run(nc, [arrays], core_ids=[0]).results[0]
    return tuple(got[f"out_{n}"] for n in outs)
```
